# Optimizing a Trainium2 kernel written in Bass

```python
import jax, jax.numpy as jnp
from jax import lax
import numpy as np

D_MODEL = 1024
BATCH = 1
SEQ = 256
DEPTH = 2

D_FF = 2816
CHUNK = 128
A_GROUPS = 4
A_GROUP_CH = 128
A_HALF = A_GROUPS * A_GROUP_CH
N_HEADS = 8
HEAD_DIM = 64
ATT_W = N_HEADS * HEAD_DIM
IDX_HEADS = 8
IDX_DIM = 64
TOPK_MAX = 256
Q_BLOCK = 128
ROPE_THETA = 10000.0
EPS = 1e-6

SPLIT_SIZES = (A_HALF, A_HALF, ATT_W, ATT_W, ATT_W, IDX_HEADS * IDX_DIM, IDX_DIM, IDX_HEADS, D_MODEL, D_MODEL)
SPLIT_POINTS = tuple(int(v) for v in np.cumsum(SPLIT_SIZES)[:-1])
N_IN = int(sum(SPLIT_SIZES))


def _rms_norm(x, g):
    xf = x.astype(jnp.float32)
    y = xf * lax.rsqrt(jnp.mean(xf * xf, axis=-1, keepdims=True) + EPS)
    return (y * g.astype(jnp.float32)).astype(x.dtype)

def _layer_norm(x, g, b):
    xf = x.astype(jnp.float32)
    mu = jnp.mean(xf, axis=-1, keepdims=True)
    var = jnp.mean(jnp.square(xf - mu), axis=-1, keepdims=True)
    y = (xf - mu) * lax.rsqrt(var + EPS)
    return (y * g.astype(jnp.float32) + b.astype(jnp.float32)).astype(x.dtype)

def _swiglu(h, w_gu, w_down):
    gate, up = jnp.split(h @ w_gu, 2, axis=-1)
    return (jax.nn.silu(gate) * up) @ w_down

def _rope(x, pos):
    d = x.shape[-1]
    inv = ROPE_THETA ** (-jnp.arange(0, d, 2, dtype=jnp.float32) / d)
    ang = pos.astype(jnp.float32)[:, None] * inv[None, :]
    cos = jnp.cos(ang)[None, :, None, :].astype(x.dtype)
    sin = jnp.sin(ang)[None, :, None, :].astype(x.dtype)
    x1, x2 = x[..., : d // 2], x[..., d // 2:]
    return jnp.concatenate([x1 * cos - x2 * sin, x2 * cos + x1 * sin], axis=-1)

def _gmlp_spatial(u, v, ln_g, ln_b, w_s, b_s):
    B, T, _ = u.shape
    u = jax.nn.gelu(u)
    v = _layer_norm(jax.nn.gelu(v), ln_g, ln_b)
    vb = v.reshape(B, T // CHUNK, CHUNK, A_GROUPS, A_GROUP_CH)
    mask = jnp.tril(jnp.ones((CHUNK, CHUNK), dtype=bool))
    ws = jnp.where(mask[None], w_s, jnp.zeros((), w_s.dtype))
    mixed = jnp.einsum('gts,bnsgc->bntgc', ws, vb) + b_s.T[:, :, None]
    return u * mixed.reshape(B, T, A_HALF)

def _dsa_attention(q, k, v, q_idx, k_idx, w_idx):
    B, T, H, Dh = q.shape
    L = k.shape[1]
    topk = min(TOPK_MAX, L // 4)
    nb = T // Q_BLOCK
    idx_scale = (IDX_DIM ** -0.5) * (IDX_HEADS ** -0.5)
    att_scale = HEAD_DIM ** -0.5
    kpos = jnp.arange(L, dtype=jnp.int32)
    qpos = jnp.arange(T, dtype=jnp.int32).reshape(nb, Q_BLOCK)
    gather = jax.vmap(lambda a, i: a[i])

    def to_blocks(a):
        return a.reshape((B, nb, Q_BLOCK) + a.shape[2:]).swapaxes(0, 1)

    def one_block(args):
        qb, qib, wb, pb = args
        logits = jnp.einsum('bqhd,bsd->bqhs', qib, k_idx).astype(jnp.float32)
        score = jnp.einsum('bqhs,bqh->bqs', jax.nn.relu(logits), wb.astype(jnp.float32)) * idx_scale
        causal = kpos[None, :] <= pb[:, None]
        score = jnp.where(causal[None], score, -jnp.inf)
        _, sel = lax.top_k(score, topk)
        k_sel = gather(k, sel)
        v_sel = gather(v, sel)
        s = jnp.einsum('bqhd,bqkhd->bhqk', qb, k_sel).astype(jnp.float32) * att_scale
        valid = sel <= pb[None, :, None]
        s = jnp.where(valid[:, None], s, -jnp.inf)
        p = jax.nn.softmax(s, axis=-1).astype(v.dtype)
        return jnp.einsum('bhqk,bqkhd->bqhd', p, v_sel)

    out = lax.map(one_block, (to_blocks(q), to_blocks(q_idx), to_blocks(w_idx), qpos))
    return out.swapaxes(0, 1).reshape(B, T, H * Dh)

def _hybrid_mixer(h, w_in, b_gate, gmlp_ln_g, gmlp_ln_b, gmlp_w_s, gmlp_b_s, w_pa, w_pb, w_out):
    B, T, _ = h.shape
    proj = h @ w_in
    u, va, q, k, v, qi, ki, wi, g_a, g_b = jnp.split(proj, SPLIT_POINTS, axis=-1)
    pos = jnp.arange(T, dtype=jnp.int32)
    y_a = _gmlp_spatial(u, va, gmlp_ln_g, gmlp_ln_b, gmlp_w_s, gmlp_b_s) @ w_pa
    q = _rope(q.reshape(B, T, N_HEADS, HEAD_DIM), pos)
    k = _rope(k.reshape(B, T, N_HEADS, HEAD_DIM), pos)
    v = v.reshape(B, T, N_HEADS, HEAD_DIM)
    qi = _rope(qi.reshape(B, T, IDX_HEADS, IDX_DIM), pos)
    ki = _rope(ki[:, :, None, :], pos)[:, :, 0, :]
    y_b = _dsa_attention(q, k, v, qi, ki, wi) @ w_pb
    gates = jax.nn.sigmoid(jnp.concatenate([g_a, g_b], axis=-1) + b_gate)
    gate_a, gate_b = jnp.split(gates, 2, axis=-1)
    return (gate_a * y_a + gate_b * y_b) @ w_out

def first_inputs(seed: int = 0) -> dict:
    key = jax.random.key(seed)
    ks = jax.random.split(key, 20)
    f32 = jnp.float32

    def nrm(k, shape, scale):
        return jax.random.normal(k, shape, f32) * scale

    def gain(k, shape):
        return 1.0 + 0.05 * jax.random.normal(k, shape, f32)

    return {
        "x": jax.random.normal(ks[0], (BATCH, SEQ, D_MODEL), f32),
        "ffn1_norm": gain(ks[1], (DEPTH, D_MODEL)),
        "ffn1_w_gu": nrm(ks[2], (DEPTH, D_MODEL, 2 * D_FF), D_MODEL ** -0.5),
        "ffn1_w_down": nrm(ks[3], (DEPTH, D_FF, D_MODEL), D_FF ** -0.5),
        "mix_norm": gain(ks[4], (DEPTH, D_MODEL)),
        "w_in": nrm(ks[5], (DEPTH, D_MODEL, N_IN), D_MODEL ** -0.5),
        "b_gate": nrm(ks[6], (DEPTH, 2 * D_MODEL), 0.02),
        "gmlp_ln_g": gain(ks[7], (DEPTH, A_HALF)),
        "gmlp_ln_b": nrm(ks[8], (DEPTH, A_HALF), 0.02),
        "gmlp_w_s": nrm(ks[9], (DEPTH, A_GROUPS, CHUNK, CHUNK), 0.5 * CHUNK ** -0.5),
        "gmlp_b_s": 1.0 + 0.1 * jax.random.normal(ks[10], (DEPTH, A_GROUPS, CHUNK), f32),
        "w_pa": nrm(ks[11], (DEPTH, A_HALF, D_MODEL), A_HALF ** -0.5),
        "w_pb": nrm(ks[12], (DEPTH, ATT_W, D_MODEL), ATT_W ** -0.5),
        "w_out": nrm(ks[13], (DEPTH, D_MODEL, D_MODEL), D_MODEL ** -0.5),
        "ffn2_norm": gain(ks[14], (DEPTH, D_MODEL)),
        "ffn2_w_gu": nrm(ks[15], (DEPTH, D_MODEL, 2 * D_FF), D_MODEL ** -0.5),
        "ffn2_w_down": nrm(ks[16], (DEPTH, D_FF, D_MODEL), D_FF ** -0.5),
        "final_norm": gain(ks[17], (D_MODEL,)),
    }

def first_block(x, ffn1_norm, ffn1_w_gu, ffn1_w_down, mix_norm, w_in, b_gate, gmlp_ln_g, gmlp_ln_b,
              gmlp_w_s, gmlp_b_s, w_pa, w_pb, w_out, ffn2_norm, ffn2_w_gu, ffn2_w_down, final_norm):
    for l in range(DEPTH):
        x = x + 0.5 * _swiglu(_rms_norm(x, ffn1_norm[l]), ffn1_w_gu[l], ffn1_w_down[l])
        x = x + _hybrid_mixer(_rms_norm(x, mix_norm[l]), w_in[l], b_gate[l], gmlp_ln_g[l], gmlp_ln_b[l],
                              gmlp_w_s[l], gmlp_b_s[l], w_pa[l], w_pb[l], w_out[l])
        x = x + 0.5 * _swiglu(_rms_norm(x, ffn2_norm[l]), ffn2_w_gu[l], ffn2_w_down[l])
    return _rms_norm(x, final_norm)


N_HEADS_2 = 4
BRANCH_WIDTH = N_HEADS_2 * HEAD_DIM
N_BRANCHES = 4
RMS_EPS = 1e-6

DSW_PATTERNS = ((128, 1), (512, 4), (2048, 16))

MLA_Q_RANK = 192
MLA_KV_RANK = 128
MLA_NOPE_DIM = 64
MLA_ROPE_DIM = 32
MLA_V_DIM = 64

NSA_CMP_BLOCK = 32
NSA_CMP_STRIDE = 16
NSA_CMP_HIDDEN = 128
NSA_SEL_BLOCK = 64
NSA_TOP_N = 16
NSA_WINDOW = 512
NSA_KV_DIM = 64
NSA_FORCE_SCORE = 1e9

N_ALIBI_HEADS = 8

IN_SPLITS = (
    ("a_q", BRANCH_WIDTH), ("a_k", BRANCH_WIDTH), ("a_v", BRANCH_WIDTH), ("a_gate", BRANCH_WIDTH),
    ("b_cq", MLA_Q_RANK), ("b_ckv", MLA_KV_RANK), ("b_kpe", MLA_ROPE_DIM), ("b_gate", BRANCH_WIDTH),
    ("c_q", BRANCH_WIDTH), ("c_kc", NSA_KV_DIM), ("c_vc", NSA_KV_DIM), ("c_ks", NSA_KV_DIM),
    ("c_vs", NSA_KV_DIM), ("c_kw", NSA_KV_DIM), ("c_vw", NSA_KV_DIM), ("c_g", 3 * N_HEADS_2),
    ("c_gate", BRANCH_WIDTH),
    ("d_q", BRANCH_WIDTH), ("d_k", BRANCH_WIDTH), ("d_v", BRANCH_WIDTH), ("d_gate", BRANCH_WIDTH),
)
D_IN = sum(w for _, w in IN_SPLITS)


def rmsnorm(x, g):
    xf = x.astype(jnp.float32)
    y = xf * lax.rsqrt(jnp.mean(xf * xf, axis=-1, keepdims=True) + RMS_EPS)
    return (y * g.astype(jnp.float32)).astype(x.dtype)

def split_columns(p):
    out, off = {}, 0
    for name, w in IN_SPLITS:
        out[name] = p[..., off:off + w]
        off += w
    return out

def alibi_slopes():
    s = 2.0 ** (-8.0 * (np.arange(N_ALIBI_HEADS) + 1) / N_ALIBI_HEADS)
    s = jnp.asarray(s, jnp.float32)
    return s[0::2], s[1::2]

def masked_softmax(s, mask):
    s = jnp.where(mask, s, -jnp.inf)
    m = jnp.max(s, axis=-1, keepdims=True)
    m = jnp.where(jnp.isfinite(m), m, 0.0)
    e = jnp.exp(s - m)
    return e / jnp.maximum(jnp.sum(e, axis=-1, keepdims=True), 1e-30)

def sweep_query_blocks(block_fn, seq):
    out = lax.map(block_fn, jnp.arange(seq // Q_BLOCK))
    nq, b, tq, h, d = out.shape
    return jnp.swapaxes(out, 0, 1).reshape(b, nq * tq, h, d)

def rope(x, pos):
    half = x.shape[-1] // 2
    inv = ROPE_THETA ** (-jnp.arange(half, dtype=jnp.float32) / half)
    ang = pos.astype(jnp.float32)[:, None] * inv[None, :]
    cos, sin = jnp.cos(ang)[:, None, :], jnp.sin(ang)[:, None, :]
    xf = x.astype(jnp.float32)
    x1, x2 = xf[..., :half], xf[..., half:]
    return jnp.concatenate([x1 * cos - x2 * sin, x1 * sin + x2 * cos], axis=-1).astype(x.dtype)

def dilated_window_attention(q, k, v, slopes):
    B, S, H, Dh = q.shape
    scale = Dh ** -0.5

    def block(qb):
        t0 = qb * Q_BLOCK
        t = t0 + jnp.arange(Q_BLOCK)
        qblk = lax.dynamic_slice_in_dim(q, t0, Q_BLOCK, axis=1)
        outs, lses = [], []
        for window, dil in DSW_PATTERNS:
            dist = dil * jnp.arange(window // dil + 1)
            idx = t[:, None] - dist[None, :]
            valid = idx >= 0
            idxc = jnp.maximum(idx, 0)
            kg, vg = k[:, idxc], v[:, idxc]
            s = jnp.einsum('bqhd,bqjhd->bhqj', qblk, kg).astype(jnp.float32) * scale
            s = s - slopes[:, None, None] * dist.astype(jnp.float32)
            s = jnp.where(valid[None, None], s, -jnp.inf)
            lse = jax.nn.logsumexp(s, axis=-1)
            p = jnp.exp(s - lse[..., None])
            outs.append(jnp.einsum('bhqj,bqjhd->bqhd', p.astype(v.dtype), vg))
            lses.append(lse)
        w = jax.nn.softmax(jnp.stack(lses, axis=0), axis=0)
        o = 0.0
        for i in range(len(DSW_PATTERNS)):
            o = o + jnp.transpose(w[i], (0, 2, 1))[..., None].astype(v.dtype) * outs[i]
        return o

    return sweep_query_blocks(block, S)

def blocked_causal_softmax(q, k, v, scale):
    B, S, H, _ = q.shape
    kpos = jnp.arange(S)

    def block(qb):
        t0 = qb * Q_BLOCK
        t = t0 + jnp.arange(Q_BLOCK)
        qblk = lax.dynamic_slice_in_dim(q, t0, Q_BLOCK, axis=1)
        s = jnp.einsum('bqhd,bkhd->bhqk', qblk, k).astype(jnp.float32) * scale
        s = jnp.where(kpos[None, :] <= t[:, None], s, -jnp.inf)
        p = jax.nn.softmax(s, axis=-1)
        return jnp.einsum('bhqk,bkhd->bqhd', p.astype(v.dtype), v)

    return sweep_query_blocks(block, S)

def mla_attention(cq, ckv, kpe, q_norm_g, w_uq, kv_norm_g, w_ukv):
    B, S, _ = cq.shape
    pos = jnp.arange(S)
    q = (rmsnorm(cq, q_norm_g) @ w_uq).reshape(B, S, N_HEADS_2, MLA_NOPE_DIM + MLA_ROPE_DIM)
    q = jnp.concatenate([q[..., :MLA_NOPE_DIM], rope(q[..., MLA_NOPE_DIM:], pos)], axis=-1)
    kv = (rmsnorm(ckv, kv_norm_g) @ w_ukv).reshape(B, S, N_HEADS_2, MLA_NOPE_DIM + MLA_V_DIM)
    k_nope, v = kv[..., :MLA_NOPE_DIM], kv[..., MLA_NOPE_DIM:]
    k_pe = rope(kpe[:, :, None, :], pos)
    k = jnp.concatenate([k_nope, jnp.broadcast_to(k_pe, (B, S, N_HEADS_2, MLA_ROPE_DIM))], axis=-1)
    return blocked_causal_softmax(q, k, v, (MLA_NOPE_DIM + MLA_ROPE_DIM) ** -0.5)

def compress_blocks(tok, pos_emb, w1, b1, w2, b2):
    B, S, Dk = tok.shape
    n_cmp = (S - NSA_CMP_BLOCK) // NSA_CMP_STRIDE + 1
    idx = np.arange(n_cmp)[:, None] * NSA_CMP_STRIDE + np.arange(NSA_CMP_BLOCK)[None, :]
    blocks = tok[:, idx] + pos_emb
    hid = jax.nn.gelu(blocks.reshape(B, n_cmp, NSA_CMP_BLOCK * Dk) @ w1 + b1)
    return hid @ w2 + b2

def nsa_attention(q, kc, vc, ks, vs, kw, vw, gates, pos_emb, w1, b1, w2, b2, slopes):
    B, S, H, Dh = q.shape
    scale = Dh ** -0.5
    k_cmp = compress_blocks(kc, pos_emb[0], w1[0], b1[0], w2[0], b2[0])
    v_cmp = compress_blocks(vc, pos_emb[1], w1[1], b1[1], w2[1], b2[1])
    n_cmp = k_cmp.shape[1]
    cmp_end = jnp.arange(n_cmp) * NSA_CMP_STRIDE + NSA_CMP_BLOCK - 1
    n_sel = S // NSA_SEL_BLOCK
    top_n = min(NSA_TOP_N, n_sel)
    r_sel, r_cmp = NSA_SEL_BLOCK // NSA_CMP_STRIDE, NSA_CMP_BLOCK // NSA_CMP_STRIDE
    src = (jnp.arange(n_sel)[:, None, None] * r_sel - jnp.arange(r_sel)[None, :, None]
           - jnp.arange(r_cmp)[None, None, :]).reshape(n_sel, -1)
    sel_map = jnp.sum(src[..., None] == jnp.arange(n_cmp), axis=1).astype(jnp.float32)
    kw_pad = jnp.pad(kw, ((0, 0), (NSA_WINDOW, 0), (0, 0)))
    vw_pad = jnp.pad(vw, ((0, 0), (NSA_WINDOW, 0), (0, 0)))
    blk = jnp.arange(n_sel)
    sel_off = jnp.arange(NSA_SEL_BLOCK)

    def block(qb):
        t0 = qb * Q_BLOCK
        t = t0 + jnp.arange(Q_BLOCK)
        qblk = lax.dynamic_slice_in_dim(q, t0, Q_BLOCK, axis=1)
        gblk = lax.dynamic_slice_in_dim(gates, t0, Q_BLOCK, axis=1)
        dist_c = (t[:, None] - cmp_end[None, :]).astype(jnp.float32)
        s = jnp.einsum('bqhd,bnd->bhqn', qblk, k_cmp).astype(jnp.float32) * scale
        p_cmp = masked_softmax(s - slopes[:, None, None] * dist_c, dist_c >= 0)
        o_cmp = jnp.einsum('bhqn,bnd->bqhd', p_cmp.astype(v_cmp.dtype), v_cmp)
        p_sel = jnp.einsum('bhqn,jn->bqj', p_cmp, sel_map)
        cur = t // NSA_SEL_BLOCK
        valid = blk[None, :] * NSA_SEL_BLOCK <= t[:, None]
        forced = (blk[None, :] == 0) | (blk[None, :] == cur[:, None]) | (blk[None, :] == cur[:, None] - 1)
        score = jnp.where(valid, jnp.where(forced, NSA_FORCE_SCORE, p_sel), -jnp.inf)
        _, sel = lax.top_k(score, top_n)
        tok = (sel[..., None] * NSA_SEL_BLOCK + sel_off).reshape(B, Q_BLOCK, top_n * NSA_SEL_BLOCK)
        ks_g = jax.vmap(lambda a, i: a[i])(ks, tok)
        vs_g = jax.vmap(lambda a, i: a[i])(vs, tok)
        dist_s = (t[None, :, None] - tok).astype(jnp.float32)
        s = jnp.einsum('bqhd,bqkd->bhqk', qblk, ks_g).astype(jnp.float32) * scale
        s = s - slopes[None, :, None, None] * dist_s[:, None]
        p = masked_softmax(s, (dist_s >= 0)[:, None])
        o_slc = jnp.einsum('bhqk,bqkd->bqhd', p.astype(vs_g.dtype), vs_g)
        kwin = lax.dynamic_slice_in_dim(kw_pad, t0, Q_BLOCK + NSA_WINDOW, axis=1)
        vwin = lax.dynamic_slice_in_dim(vw_pad, t0, Q_BLOCK + NSA_WINDOW, axis=1)
        spos = t0 - NSA_WINDOW + jnp.arange(Q_BLOCK + NSA_WINDOW)
        dist_w = t[:, None] - spos[None, :]
        mask_w = (dist_w >= 0) & (dist_w < NSA_WINDOW) & (spos[None, :] >= 0)
        s = jnp.einsum('bqhd,bkd->bhqk', qblk, kwin).astype(jnp.float32) * scale
        p = masked_softmax(s - slopes[:, None, None] * dist_w.astype(jnp.float32), mask_w)
        o_win = jnp.einsum('bhqk,bkd->bqhd', p.astype(vwin.dtype), vwin)
        return gblk[..., 0:1] * o_cmp + gblk[..., 1:2] * o_slc + gblk[..., 2:3] * o_win

    return sweep_query_blocks(block, S)

def stick_breaking_attention(q, k, v):
    B, S, H, Dh = q.shape
    scale = Dh ** -0.5
    kpos = jnp.arange(S)

    def block(qb):
        t0 = qb * Q_BLOCK
        t = t0 + jnp.arange(Q_BLOCK)
        qblk = lax.dynamic_slice_in_dim(q, t0, Q_BLOCK, axis=1)
        z = jnp.einsum('bqhd,bkhd->bhqk', qblk, k).astype(jnp.float32) * scale
        mask = kpos[None, :] < t[:, None]
        log1m = jnp.where(mask, jax.nn.log_sigmoid(-z), 0.0)
        after = lax.cumsum(log1m, axis=3, reverse=True) - log1m
        a = jnp.where(mask, jnp.exp(jax.nn.log_sigmoid(z) + after), 0.0)
        return jnp.einsum('bhqk,bkhd->bqhd', a.astype(v.dtype), v)

    return sweep_query_blocks(block, S)

def second_inputs(seed: int = 0) -> dict:
    key = jax.random.key(seed)
    ks = jax.random.split(key, 18)
    f32 = jnp.float32

    def nrm(k, shape, fan_in):
        return jax.random.normal(k, shape, f32) * (fan_in ** -0.5)

    def gain(k, shape):
        return 1.0 + 0.05 * jax.random.normal(k, shape, f32)

    return {
        "x": jax.random.normal(ks[0], (BATCH, SEQ, D_MODEL), f32),
        "norm_g": gain(ks[1], (DEPTH, D_MODEL)),
        "w_in": nrm(ks[2], (DEPTH, D_MODEL, D_IN), D_MODEL),
        "mla_q_norm": gain(ks[3], (DEPTH, MLA_Q_RANK)),
        "mla_w_uq": nrm(ks[4], (DEPTH, MLA_Q_RANK, N_HEADS_2 * (MLA_NOPE_DIM + MLA_ROPE_DIM)), MLA_Q_RANK),
        "mla_kv_norm": gain(ks[5], (DEPTH, MLA_KV_RANK)),
        "mla_w_ukv": nrm(ks[6], (DEPTH, MLA_KV_RANK, N_HEADS_2 * (MLA_NOPE_DIM + MLA_V_DIM)), MLA_KV_RANK),
        "nsa_pos": 0.1 * jax.random.normal(ks[7], (DEPTH, 2, NSA_CMP_BLOCK, NSA_KV_DIM), f32),
        "nsa_w1": nrm(ks[8], (DEPTH, 2, NSA_CMP_BLOCK * NSA_KV_DIM, NSA_CMP_HIDDEN), NSA_CMP_BLOCK * NSA_KV_DIM),
        "nsa_b1": 0.02 * jax.random.normal(ks[9], (DEPTH, 2, NSA_CMP_HIDDEN), f32),
        "nsa_w2": nrm(ks[10], (DEPTH, 2, NSA_CMP_HIDDEN, NSA_KV_DIM), NSA_CMP_HIDDEN),
        "nsa_b2": 0.02 * jax.random.normal(ks[11], (DEPTH, 2, NSA_KV_DIM), f32),
        "w_branch": nrm(ks[12], (DEPTH, N_BRANCHES, BRANCH_WIDTH, D_MODEL), BRANCH_WIDTH),
        "w_merge": nrm(ks[13], (DEPTH, N_BRANCHES, D_MODEL, D_MODEL), D_MODEL),
        "b_merge": 0.02 * jax.random.normal(ks[14], (DEPTH, N_BRANCHES, D_MODEL), f32),
        "w_out": nrm(ks[15], (DEPTH, D_MODEL, D_MODEL), D_MODEL),
        "final_norm_g": gain(ks[16], (D_MODEL,)),
    }

def second_block(x, norm_g, w_in, mla_q_norm, mla_w_uq, mla_kv_norm, mla_w_ukv, nsa_pos, nsa_w1,
              nsa_b1, nsa_w2, nsa_b2, w_branch, w_merge, b_merge, w_out, final_norm_g):
    B, S, D = x.shape
    slopes_a, slopes_c = alibi_slopes()
    for l in range(DEPTH):
        h = rmsnorm(x, norm_g[l])
        c = split_columns(h @ w_in[l])
        heads = lambda a: a.reshape(B, S, N_HEADS_2, HEAD_DIM)
        flat = lambda a: a.reshape(B, S, BRANCH_WIDTH)
        y_a = flat(dilated_window_attention(heads(c["a_q"]), heads(c["a_k"]), heads(c["a_v"]), slopes_a))
        y_a = y_a * jax.nn.silu(c["a_gate"])
        y_b = flat(mla_attention(c["b_cq"], c["b_ckv"], c["b_kpe"], mla_q_norm[l], mla_w_uq[l],
                                 mla_kv_norm[l], mla_w_ukv[l]))
        y_b = y_b * jax.nn.silu(c["b_gate"])
        g_c = jax.nn.sigmoid(c["c_g"]).reshape(B, S, N_HEADS_2, 3)
        y_c = flat(nsa_attention(heads(c["c_q"]), c["c_kc"], c["c_vc"], c["c_ks"], c["c_vs"],
                                 c["c_kw"], c["c_vw"], g_c, nsa_pos[l], nsa_w1[l], nsa_b1[l],
                                 nsa_w2[l], nsa_b2[l], slopes_c))
        y_c = y_c * jax.nn.silu(c["c_gate"])
        y_d = flat(stick_breaking_attention(heads(c["d_q"]), heads(c["d_k"]), heads(c["d_v"])))
        y_d = y_d * jax.nn.silu(c["d_gate"])
        merged = 0.0
        for i, y in enumerate((y_a, y_b, y_c, y_d)):
            gate = jax.nn.sigmoid(h @ w_merge[l, i] + b_merge[l, i])
            merged = merged + gate * (y @ w_branch[l, i])
        x = x + merged @ w_out[l]
    return rmsnorm(x, final_norm_g)


def setup_inputs(seed=0):
    out = dict(first_inputs(seed))
    for name, value in second_inputs(seed + 1).items():
        if name != "x":
            out[name + "_2"] = value
    return out


def reference(
    x, ffn1_norm, ffn1_w_gu, ffn1_w_down, mix_norm, w_in, b_gate, gmlp_ln_g, gmlp_ln_b,
    gmlp_w_s, gmlp_b_s, w_pa, w_pb, w_out, ffn2_norm, ffn2_w_gu, ffn2_w_down, final_norm,
    norm_g_2, w_in_2, mla_q_norm_2, mla_w_uq_2, mla_kv_norm_2, mla_w_ukv_2, nsa_pos_2, nsa_w1_2,
    nsa_b1_2, nsa_w2_2, nsa_b2_2, w_branch_2, w_merge_2, b_merge_2, w_out_2, final_norm_g_2,
):
    x = first_block(
        x, ffn1_norm, ffn1_w_gu, ffn1_w_down, mix_norm, w_in, b_gate, gmlp_ln_g, gmlp_ln_b,
        gmlp_w_s, gmlp_b_s, w_pa, w_pb, w_out, ffn2_norm, ffn2_w_gu, ffn2_w_down, final_norm,
    )
    return second_block(
        x, norm_g_2, w_in_2, mla_q_norm_2, mla_w_uq_2, mla_kv_norm_2, mla_w_ukv_2, nsa_pos_2,
        nsa_w1_2, nsa_b1_2, nsa_w2_2, nsa_b2_2, w_branch_2, w_merge_2, b_merge_2, w_out_2,
        final_norm_g_2,
    )


_drawn_inputs = setup_inputs


def setup_inputs(seed=0):
    import zlib

    import numpy as np

    out = dict(_drawn_inputs(seed))
    spreads = {}
    factors = {'b_gate': 7.769,
     'gmlp_ln_g': 4.687,
     'gmlp_ln_b': 8.0,
     'mla_q_norm_2': 8.0,
     'mla_kv_norm_2': 7.045,
     'nsa_pos_2': 4.08,
     'nsa_b1_2': 8.0,
     'nsa_b2_2': 8.0,
     'b_merge_2': 8.0}
    for name, (base, spread) in spreads.items():
        noise = np.random.default_rng([zlib.crc32(name.encode()), seed]).standard_normal(out[name].shape)
        drawn = base * np.exp(spread * noise) if base else spread * noise
        out[name] = __import__('jax').numpy.asarray(drawn.astype(out[name].dtype))
    for name, factor in factors.items():
        out[name] = (out[name] * factor).astype(out[name].dtype)
    return out
```

```python
from contextlib import ExitStack

import numpy as np

import concourse.bass as bass
from concourse import mybir

ALU = mybir.AluOpType
ACT = mybir.ActivationFunctionType
AX = mybir.AxisListType
F32 = mybir.dt.float32

P = 128
D = 1024
T = 256
TT = T // P
DEPTH = 2
DK = D // P
FF = 2816
FK = FF // P
EPS = 1e-6
NEG = -1e30
TAKEN = -3e38
PACK = 384
HD = 64
BW = 256
TOPK = 64
NCMP = 15

FFN_STEPS = [DK * 512] * 11 + [FK * 256] * 4
PROJ1_STEPS = [DK * 512] * 6 + [DK * 128] + [DK * 8]
MERGE1_STEPS = [24 * 256] * 4
OUT_STEPS = [DK * 512] * 2
STEPS1 = FFN_STEPS + PROJ1_STEPS + MERGE1_STEPS + OUT_STEPS + FFN_STEPS
C2_COLS = 396
PROJ2_STEPS = [DK * 512, DK * 512, DK * 352, DK * 512, DK * 512, DK * C2_COLS, DK * 512, DK * 512,
               2 * 384 + 512, 2 * 16 * 128 + 256]
MERGE2_STEPS = [20 * 256] * 8
STEPS2 = PROJ2_STEPS + MERGE2_STEPS + OUT_STEPS
SLOT = max(STEPS1 + STEPS2)
W1_TOTAL, W2_TOTAL = sum(STEPS1), sum(STEPS2)


def sections(widths):
    at, out = 0, {}
    for name, w in widths:
        out[name] = (at, at + w)
        at += w
    return out, at


CONST, NCONST = sections([
    ("ident", P), ("swap64", P), ("swap96", 96), ("cos64", T), ("sin64", T), ("cos96", T), ("sin96", T),
    ("causal", PACK), ("alibi_a", 4 * PACK), ("alibi_c", 4 * PACK), ("alibi_cmp", 4 * TT * NCMP),
    ("upto", P), ("before", PACK), ("later", P)])
PAR1, NPAR1 = sections([("g_ffn1", DK), ("g_mix", DK), ("g_ffn2", DK), ("b_gate", 2 * DK),
                        ("ln_g", 512), ("ln_b", 512), ("b_s", 512), ("w_s", 512)])
PAR2, NPAR2 = sections([("g_norm", DK), ("b_merge", 4 * DK), ("g_q", 2), ("g_kv", 1), ("b1", 2),
                        ("b2_k", 1), ("pos", 32), ("b2_v", HD)])
FIN, NFIN = sections([("final1", DK), ("final2", DK)])


def build(nc, x_in, w1_in, w2_in, par1_in, par2_in, fin_in, const_in, out):
    ctx = ExitStack()
    with ctx:
        def sb(name, shape):
            return ctx.enter_context(nc.sbuf_tensor(name, shape, F32))

        ring = sb("ring", [P, 2, SLOT])
        xT = sb("xT", [P, DK, T])
        hT = sb("hT", [P, DK, T])
        con = sb("con", [P, NCONST])
        par1 = sb("par1", [P, NPAR1])
        par2 = sb("par2", [P, NPAR2])
        fin = sb("fin", [P, NFIN])
        ones = sb("ones", [P, P])
        stat = sb("stat", [P, 3, T])
        WORK = 18800
        work = sb("work", [P, WORK])
        ps = ctx.enter_context(nc.psum_tensor("ps", [P, 8, 512], F32))

        def area(at, *shape):
            n = int(np.prod(shape))
            assert at + n <= WORK, (at, n)
            v = work[:, at:at + n]
            if len(shape) == 2:
                v = v.rearrange("p (a b) -> p a b", a=shape[0])
            if len(shape) == 3:
                v = v.rearrange("p (a b c) -> p a b c", a=shape[0], b=shape[1])
            return v, at + n

        def const(name, h=None):
            a, b = CONST[name]
            v = con[:, a:b]
            return v if h is None else v.rearrange("p (h n) -> p h n", h=h)

        def p1(name):
            a, b = PAR1[name]
            return par1[:, a:b]

        def p2(name):
            a, b = PAR2[name]
            return par2[:, a:b]

        raw, e = area(0, 2, T)
        rope_a, e = area(e, T)
        rope_b, e = area(e, T)
        probs, e = area(e, 4, PACK)
        probsT, e = area(e, 4, PACK)
        negmax, e = area(e, TT, 4)
        sums, e = area(e, TT, 4)
        common = e
        squares, _ = area(0, DK, T)
        zT, e = area(0, DK, T)
        sig, e = area(e, 4, T)
        gated, e = area(e, 4, T)
        assert e <= common
        hidden, e = area(common, FK, T)
        silu_g, e = area(e, 2, T)
        uT, e = area(common, 4, T)
        yaT = uT
        rot, e = area(e, 13, T)
        v_tok, e = area(e, TT, 512)
        va_tok, e = area(e, TT, 512)
        wi_tok, e = area(e, TT, 8)
        ybT, e = area(e, 4, T)
        relu, e = area(e, 4, PACK)
        score, e = area(e, PACK)
        top8, e = area(e, 8)
        keyset, e = area(e, PACK)
        small, e = area(e, 24)
        a_qkT, e = area(common, 4, T)
        c_qkT, e = area(e, 4, T)
        d_qkT, e = area(e, 4, T)
        b_qT, e = area(e, 4, T)
        b_kT, e = area(e, 4, T)
        a_v, e = area(e, TT, BW)
        b_v, e = area(e, TT, BW)
        d_v, e = area(e, TT, BW)
        c_vg, e = area(e, TT, P)
        c_g, e = area(e, TT, 12)
        gateT = []
        for _ in range(4):
            g, e = area(e, 2, T)
            gateT.append(g)
        cmp_hidden, e = area(e, 2, NCMP)
        k_cmpT, e = area(e, NCMP)
        v_cmp, e = area(e, HD)
        cmp_b, e = area(e, 2)
        cmp_m, e = area(e, 8)
        cmp_p, e = area(e, 4 * TT * NCMP)
        keep = e + e % 2
        cqT, e = area(keep, 2, T)
        ckvT, e = area(e, T)
        kpeT, e = area(e, T)
        latent_sq, e = area(e, 3, T)
        latent_r, e = area(e, 2, T)
        cmpT, e = area(e, 2, T)
        cmp_pT, e = area(keep, 4, T)
        stick_a = probs
        stick_b, e = area(keep, 4, PACK)
        stick_log, e = area(e, 4, PACK)
        yT = []
        for _ in range(4):
            y, e = area(e, 2, T)
            yT.append(y)

        dma = ctx.enter_context(nc.semaphore("consts_landed"))
        with nc.Block() as block:
            @block.sync
            def _(sp):
                sp.dma_start(xT[:, :, :], x_in).then_inc(dma, 16)
                sp.dma_start(con[:, :], const_in).then_inc(dma, 16)
                sp.dma_start(fin[:, :], fin_in).then_inc(dma, 16)
                sp.wait_ge(dma, 48)

            @block.vector
            def _(dve):
                nc.vector.memset(ones[:, :], 1.0)

        def product(bank, slot, off, stride, c0, m, rhs, kt, rows=None):
            for k in range(kt):
                r = P if rows is None else rows[k]
                a = off + k * stride + c0
                mm = nc.tensor.matmul(bank, ring[0:r, slot, a:a + m], rhs(k)[0:r],
                                      start=(k == 0), stop=(k == kt - 1))
            return mm

        def product_tok(bank, slot, off, stride, c0, n, lhs, kt):
            for k in range(kt):
                a = off + k * stride + c0
                mm = nc.tensor.matmul(bank, lhs(k), ring[:, slot, a:a + n],
                                      start=(k == 0), stop=(k == kt - 1))
            return mm

        class Chain:

            def __init__(self, eng, sem):
                self.eng, self.sem, self.n = eng, sem, 0

            def link(self, ins):
                ins.then_inc(self.sem, 1)
                self.n += 1
                self.eng.wait_ge(self.sem, self.n)

        class Layer:

            def __init__(self, stack, steps, per_step, w_in, par, par_in, l):
                self.stack, self.sems = stack, {}
                self.steps, self.per_step = steps, per_step
                self.starts = np.concatenate([[0], np.cumsum(steps)]).tolist()
                self.tiles_before = np.concatenate([[0], np.cumsum(per_step)]).tolist()
                self.w_in, self.par, self.par_in, self.l = w_in, par, par_in, l
                for name in ("slot0_landed", "slot1_landed", "tiles_done", "act_took", "dve_took", "stage_end"):
                    self.sem(name)
                self.slot_landed = [self.sem("slot0_landed"), self.sem("slot1_landed")]

            def sem(self, name):
                if name not in self.sems:
                    self.sems[name] = self.stack.enter_context(nc.semaphore(name))
                return self.sems[name]

            def landed(self, pe, n, i=0):
                pe.wait_ge(self.slot_landed[n % 2], 16 * (n // 2 + 1) + 16 * i)

            def end_stage(self, eng, k):
                eng.drain().then_inc(self.sem("stage_end"), 1)
                eng.wait_ge(self.sem("stage_end"), 3 * k)

            def clear(self):
                nums = [s.num for s in self.sems.values()]
                nc.all_engine_barrier(sems_to_clear=range(min(nums), max(nums) + 1))

        def stream(sp, L):
            def load(n):
                sp.dma_start(ring[:, n % 2, 0:L.steps[n]], L.w_in[L.l, :, L.starts[n]:L.starts[n + 1]]
                             ).then_inc(L.slot_landed[n % 2], 16)

            sp.dma_start(L.par[:, :], L.par_in[L.l]).then_inc(L.sem("params_landed"), 16)
            load(0)
            load(1)
            n = 2
            while n < len(L.steps):
                size, per, pairs = L.steps[n], L.per_step[n - 2], 0
                while (L.steps[n:n + 2 * pairs + 2] == [size] * (2 * pairs + 2)
                       and L.per_step[n - 2:n + 2 * pairs] == [per] * (2 * pairs + 2)):
                    pairs += 1
                if pairs >= 2:
                    with sp.Fori(0, pairs) as i:
                        for j in range(2):
                            sp.wait_ge(L.sem("tiles_done"), L.tiles_before[n + j - 1] + 2 * per * i)
                            sp.dma_start(ring[:, (n + j) % 2, 0:size],
                                         L.w_in[L.l, :, bass.ds(L.starts[n + j] + 2 * size * i, size)]
                                         ).then_inc(L.slot_landed[(n + j) % 2], 16)
                    n += 2 * pairs
                else:
                    sp.wait_ge(L.sem("tiles_done"), L.tiles_before[n - 1])
                    load(n)
                    n += 1

        def norm_pe(pe, L, name):
            for k in range(DK):
                pe.wait_ge(L.sem("squared_" + name), k + 1)
                mm = nc.tensor.matmul(ps[:, 7, 0:T], ones[:, :], squares[:, k, :], start=(k == 0), stop=(k == DK - 1))
            mm.then_inc(L.sem("summed_" + name), 1)

        def norm_act(act, L, name):
            for k in range(DK):
                nc.scalar.activation(squares[:, k, :], xT[:, k, :], ACT.Square).then_inc(L.sem("squared_" + name), 1)
            act.wait_ge(L.sem("mean_" + name), 1)
            nc.scalar.activation(stat[:, 1, :], stat[:, 0, :], ACT.Sqrt).then_inc(L.sem("root_" + name), 1)

        def norm_dve(dve, L, chain, name, gain, dst):
            dve.wait_ge(L.sem("summed_" + name), 1)
            nc.vector.tensor_scalar(stat[:, 0, :], ps[:, 7, 0:T], 1.0 / D, EPS, ALU.mult, ALU.add
                                    ).then_inc(L.sem("mean_" + name), 1)
            dve.wait_ge(L.sem("root_" + name), 1)
            chain.link(nc.vector.reciprocal(stat[:, 2, :], stat[:, 1, :]))
            for k in range(DK):
                nc.vector.scalar_tensor_tensor(dst[:, k, :], xT[:, k, :], gain[:, k:k + 1], stat[:, 2, :],
                                               ALU.mult, ALU.mult).then_inc(L.sem("normed_" + name), 1)

        def ffn_pe(pe, L, n0, a0, v0, name):
            done, act_took, dve_took = L.sem("tiles_done"), L.sem("act_took"), L.sem("dve_took")
            h = lambda k: hT[:, k, :]

            def up_step(i, j, first=False):
                s, slot = 2 * i + j, (n0 + j) % 2
                L.landed(pe, n0 + j, i)
                for nt in range(2):
                    if not first:
                        pe.wait_ge(act_took, a0 + 2 * s + nt - 1)
                    product(ps[:, 2 * nt, 0:T], slot, 0, 512, nt * P, P, h, DK).then_inc(done, 1)
                    if not first:
                        pe.wait_ge(dve_took, v0 + 2 * s + nt - 1)
                    product(ps[:, 2 * nt + 1, 0:T], slot, 0, 512, 256 + nt * P, P, h, DK).then_inc(done, 1)

            pe.wait_ge(L.sem("normed_" + name), DK)
            up_step(0, 0, first=True)
            up_step(0, 1)
            with pe.Fori(1, 5) as i:
                up_step(i, 0)
                up_step(i, 1)
            up_step(5, 0)

            with pe.Fori(0, 2) as i:
                for j in range(2):
                    L.landed(pe, n0 + 11 + j, i)
                    for nt in range(2):
                        pe.wait_ge(dve_took, v0 + FK + (2 * j + nt - 1 if j else 0) + 4 * i)
                        product(ps[:, 4 + nt, 0:T], (n0 + 11 + j) % 2, 0, 256, nt * P, P,
                                lambda k: hidden[:, k, :], FK).then_inc(done, 1)

        def ffn_act(act, L, t0, v0):
            def up_step(i, j, first=False):
                s = 2 * i + j
                for nt in range(2):
                    act.wait_ge(L.sem("tiles_done"), t0 + 4 * s + 2 * nt + 1)
                    if not first:
                        act.wait_ge(L.sem("dve_took"), v0 + 2 * s + nt - 1)
                    nc.scalar.activation(silu_g[:, nt, :], ps[:, 2 * nt, 0:T], ACT.Silu
                                         ).then_inc(L.sem("act_took"), 1)

            up_step(0, 0, first=True)
            up_step(0, 1)
            with act.Fori(1, 5) as i:
                up_step(i, 0)
                up_step(i, 1)
            up_step(5, 0)

        def ffn_dve(dve, L, t0, a0):
            def up_step(i, j):
                s = 2 * i + j
                for nt in range(2):
                    dve.wait_ge(L.sem("tiles_done"), t0 + 4 * s + 2 * nt + 2)
                    dve.wait_ge(L.sem("act_took"), a0 + 2 * s + nt + 1)
                    nc.vector.tensor_tensor(hidden[:, bass.ds(2 * s + nt, 1), :], silu_g[:, nt:nt + 1, :],
                                            ps[:, 2 * nt + 1:2 * nt + 2, 0:T], ALU.mult).then_inc(L.sem("dve_took"), 1)

            with dve.Fori(0, 5) as i:
                up_step(i, 0)
                up_step(i, 1)
            up_step(5, 0)
            with dve.Fori(0, 4) as c:
                for nt in range(2):
                    dve.wait_ge(L.sem("tiles_done"), t0 + 44 + 2 * c + nt + 1)
                    xs = xT[:, bass.ds(2 * c + nt, 1), :]
                    nc.vector.scalar_tensor_tensor(xs, ps[:, 4 + nt:5 + nt, 0:T], 0.5, xs, ALU.mult, ALU.add
                                                   ).then_inc(L.sem("dve_took"), 1)

        def out_pe(pe, L, n0, v0):
            for j in range(2):
                L.landed(pe, n0 + j)
                for nt in range(4):
                    if j:
                        pe.wait_ge(L.sem("dve_took"), v0 + nt + 1)
                    product(ps[:, nt, 0:T], (n0 + j) % 2, 0, 512, nt * P, P, lambda k: zT[:, k, :], DK
                            ).then_inc(L.sem("tiles_done"), 1)

        def out_dve(dve, L, t0):
            for n in range(DK):
                dve.wait_ge(L.sem("tiles_done"), t0 + n + 1)
                nc.vector.tensor_tensor(xT[:, n, :], ps[:, n % 4, 0:T], xT[:, n, :], ALU.add
                                        ).then_inc(L.sem("dve_took"), 1)

        def rope_pe(pe, L, r, raw_count, m, swap):
            pe.wait_ge(L.sem("act_took"), raw_count)
            if r >= 2:
                pe.wait_ge(L.sem("turned_taken"), r - 1)
            nc.tensor.matmul(ps[0:m, 6 + r % 2, 0:T], swap, raw[0:m, r % 2, :], start=True, stop=True
                             ).then_inc(L.sem("turned"), 1)

        def rope_dve(dve, L, chain, r, raw_count, m, cos, sin, dst):
            dve.wait_ge(L.sem("act_took"), raw_count)
            chain.link(nc.vector.tensor_tensor(rope_a[0:m, :], raw[0:m, r % 2, :], cos, ALU.mult))
            dve.wait_ge(L.sem("turned"), r + 1)
            nc.vector.tensor_tensor(rope_b[0:m, :], ps[0:m, 6 + r % 2, 0:T], sin, ALU.mult
                                    ).then_inc(L.sem("turned_taken"), 1)
            dve.wait_ge(L.sem("turned_taken"), r + 1)
            chain.link(nc.vector.tensor_tensor(dst, rope_a[0:m, :], rope_b[0:m, :], ALU.add))

        HALVES = ((0, P), (P, PACK))

        def scores_pe(pe, L, u, q, k):
            if u:
                pe.wait_ge(L.sem("scores_taken"), u)
            for h in range(4):
                nc.tensor.matmul(ps[:, h, 0:P], q(h)[:, 0:P], k(h)[:, 0:P], start=True, stop=True)
                mm = nc.tensor.matmul(ps[:, h, P:PACK], q(h)[:, P:T], k(h)[:, 0:T], start=True, stop=True)
            mm.then_inc(L.sem("scores_ready"), 1)

        def mix_pe(pe, L, u, v):
            pe.wait_ge(L.sem("probs_ready"), u + 1)
            if u:
                pe.wait_ge(L.sem("mixed_taken"), u)
            for h in range(4):
                for a in range(0, PACK, P):
                    mm = nc.tensor.transpose(ps[:, 4 + h, a:a + P], probs[:, h, a:a + P], const("ident"))
            mm.then_inc(L.sem("probsT_ready"), 1)
            pe.wait_ge(L.sem("probsT_copied"), u + 1)
            mix_values(v).then_inc(L.sem("mixed"), 1)

        def mix_values(v):
            for h in range(4):
                o = HD * (h % 2)
                nc.tensor.matmul(ps[o:o + HD, 4 + h // 2, 0:T], v(0, h), probsT[:, h, 0:T], start=True, stop=False)
                mm = nc.tensor.matmul(ps[o:o + HD, 4 + h // 2, P:T], v(1, h), probsT[:, h, T:PACK],
                                      start=False, stop=True)
            return mm

        def soft_act(act, L, u):
            act.wait_ge(L.sem("negmax_ready"), u + 1)
            for h in range(4):
                for t, (a, b) in enumerate(HALVES):
                    nc.scalar.activation(probs[:, h, a:b], probs[:, h, a:b], ACT.Exp, bias=negmax[:, t, h:h + 1],
                                         accum_out=sums[:, t, h:h + 1]).then_inc(L.sem("exps_ready"), 1)
            act.wait_ge(L.sem("probsT_ready"), u + 1)
            nc.scalar.activation(probsT[:, :, :], ps[:, 4:8, 0:PACK], ACT.Copy).then_inc(L.sem("probsT_copied"), 1)

        def soft_dve(dve, L, chain, u, scale, bias, gate=None):
            dve.wait_ge(L.sem("scores_ready"), u + 1)
            if u:
                dve.wait_ge(L.sem("probsT_ready"), u)
            nc.vector.scalar_tensor_tensor(probs[:, :, :], ps[:, 0:4, 0:PACK], scale, bias, ALU.mult, ALU.add
                                           ).then_inc(L.sem("scores_taken"), 1)
            dve.wait_ge(L.sem("scores_taken"), u + 1)
            chain.link(nc.vector.reduce_max(negmax[:, 0, :], probs[:, :, 0:P], AX.X, negate=True))
            nc.vector.reduce_max(negmax[:, 1, :], probs[:, :, P:PACK], AX.X, negate=True
                                 ).then_inc(L.sem("negmax_ready"), 1)
            dve.wait_ge(L.sem("exps_ready"), 8 * u + 8)
            chain.link(nc.vector.reciprocal(sums[:, :, :], sums[:, :, :]))
            if gate is not None:
                chain.link(nc.vector.tensor_tensor(sums[:, :, :], sums[:, :, :], gate, ALU.mult))
            for t, (a, b) in enumerate(HALVES):
                r = sums[:, t, :].rearrange("p (h o) -> p h o", o=1).to_broadcast([P, 4, b - a])
                ins = nc.vector.tensor_tensor(probs[:, :, a:b], probs[:, :, a:b], r, ALU.mult)
                if t == 0:
                    chain.link(ins)
            ins.then_inc(L.sem("probs_ready"), 1)

        def first_layer(l):
            with ExitStack() as stack:
                L = Layer(stack, STEPS1,
                          [4] * 11 + [2] * 4 + [4, 2, 4, 4, 4, 2, 1, 2] + [8] * 4 + [4, 4] + [4] * 11 + [2] * 4,
                          w1_in, par1, par1_in, l)
                tb = L.tiles_before
                PROJ, MERGE, OUT, FFN2 = 15, 23, 27, 29
                proj_a, proj_v = 22, 30
                merge_a, merge_v = proj_a + 23, proj_v
                out_v = merge_v + 16
                ffn2_a, ffn2_v = merge_a + 16, out_v + 8
                TILES = ([("u", n) for n in range(4)] + [("va", t) for t in range(TT)] + [("q", n) for n in range(4)]
                         + [("k", n) for n in range(4)] + [("qi", n) for n in range(4)]
                         + [("v", t) for t in range(TT)] + [("ki", 0)] + [("wi", t) for t in range(TT)])
                STEP = {"u": 0, "va": 1, "q": 2, "k": 3, "qi": 4, "v": 5, "ki": 6, "wi": 7}
                ROT = {"q": 0, "k": 4, "qi": 8, "ki": 12}
                ropes = [i for i, (kind, _) in enumerate(TILES) if kind in ROT]
                idx_scale = 64 ** -0.5 * 8 ** -0.5

                def head(base, h):
                    return rot[HD * (h % 2):HD * (h % 2) + HD, base + h // 2, :]

                block = stack.enter_context(nc.Block())

                @block.sync
                def _(sp):
                    stream(sp, L)

                @block.tensor
                def _(pe):
                    pe.wait_ge(L.sem("params_landed"), 16)
                    norm_pe(pe, L, "ffn1")
                    ffn_pe(pe, L, 0, 0, 0, "ffn1")
                    L.end_stage(pe, 1)

                    norm_pe(pe, L, "mix")
                    pe.wait_ge(L.sem("normed_mix"), DK)
                    for i, (kind, n) in enumerate(TILES):
                        s, b = PROJ + STEP[kind], i % 6
                        if n == 0:
                            L.landed(pe, s)
                        if i >= 6:
                            pe.wait_ge(L.sem("act_took"), proj_a + i - 5)
                        if kind in ("u", "q", "k", "qi"):
                            mm = product(ps[:, b, 0:T], s % 2, 0, 512, n * P, P, lambda k: hT[:, k, :], DK)
                        elif kind == "ki":
                            mm = product(ps[:, b, 0:T], s % 2, 0, P, 0, P, lambda k: hT[:, k, :], DK)
                        else:
                            w = 8 if kind == "wi" else 512
                            mm = product_tok(ps[:, b, 0:w], s % 2, 0, w, 0, w, lambda k: hT[:, k, n * P:n * P + P], DK)
                        mm.then_inc(L.sem("tiles_done"), 1)
                        if i - 1 in ropes:
                            rope_pe(pe, L, ropes.index(i - 1), proj_a + i, P, const("swap64"))
                    L.end_stage(pe, 2)

                    for h in range(8):
                        if h >= 4:
                            pe.wait_ge(L.sem("logits_taken"), h - 3)
                        o = HD * (h % 2)
                        nc.tensor.matmul(ps[:, h % 4, 0:P], head(8, h)[:, 0:P], rot[o:o + HD, 12, 0:P],
                                         start=True, stop=True)
                        nc.tensor.matmul(ps[:, h % 4, P:PACK], head(8, h)[:, P:T], rot[o:o + HD, 12, :],
                                         start=True, stop=True).then_inc(L.sem("logits_ready"), 1)
                    pe.wait_ge(L.sem("gate_normed"), 2)
                    for g in range(4):
                        for c in range(TT):
                            mm = nc.tensor.matmul(ps[:, 4 + g, c * P:c * P + P], va_tok[:, c, g * P:g * P + P],
                                                  p1("w_s")[:, g * P:g * P + P], start=True, stop=True)
                    mm.then_inc(L.sem("tokens_mixed"), 1)
                    pe.wait_ge(L.sem("logits_taken"), 8)
                    pe.wait_ge(L.sem("tokens_taken"), 1)
                    for u in range(2):
                        scores_pe(pe, L, u, lambda h: head(0, 4 * u + h), lambda h: head(4, 4 * u + h))
                        mix_pe(pe, L, u, lambda t, h: v_tok[:, t, (4 * u + h) * HD:(4 * u + h + 1) * HD])
                    L.end_stage(pe, 3)

                    def merge_tile(i, jj, first=False):
                        j, st, nt = 4 * i + jj, jj // 2, jj % 2
                        if nt == 0:
                            L.landed(pe, MERGE + st, i)
                        for q, (off, kt, src) in enumerate(((0, 8, hT), (16, 4, yaT), (8, 8, hT), (20, 4, ybT))):
                            if not first:
                                took, base = ("dve_took", merge_v) if q % 2 else ("act_took", merge_a)
                                pe.wait_ge(L.sem(took), base + 2 * j - 3 + q // 2)
                            product(ps[:, 4 * nt + q, 0:T], (MERGE + st) % 2, off * 256, 256, nt * P, P,
                                    lambda k: src[:, k, :], kt).then_inc(L.sem("tiles_done"), 1)

                    for i in range(2):
                        for jj in range(4):
                            merge_tile(i, jj, first=(i == 0 and jj < 2))
                    pe.wait_ge(L.sem("z_ready"), DK)
                    out_pe(pe, L, OUT, out_v)
                    L.end_stage(pe, 4)

                    norm_pe(pe, L, "ffn2")
                    ffn_pe(pe, L, FFN2, ffn2_a, ffn2_v, "ffn2")
                    L.end_stage(pe, 5)

                @block.scalar
                def _(act):
                    norm_act(act, L, "ffn1")
                    ffn_act(act, L, 0, 0)
                    L.end_stage(act, 1)

                    norm_act(act, L, "mix")
                    for i, (kind, n) in enumerate(TILES):
                        act.wait_ge(L.sem("tiles_done"), tb[PROJ] + i + 1)
                        b = i % 6
                        if kind == "u":
                            ins = nc.scalar.activation(uT[:, n, :], ps[:, b, 0:T], ACT.Gelu_apprx_tanh)
                        elif kind == "va":
                            ins = nc.scalar.activation(va_tok[:, n, :], ps[:, b, :], ACT.Gelu_apprx_tanh)
                        elif kind == "v":
                            ins = nc.scalar.activation(v_tok[:, n, :], ps[:, b, :], ACT.Copy)
                        elif kind == "wi":
                            ins = nc.scalar.activation(wi_tok[:, n, :], ps[:, b, 0:8], ACT.Copy, scale=idx_scale)
                        else:
                            r = ropes.index(i)
                            if r >= 2:
                                act.wait_ge(L.sem("turned_taken"), r - 1)
                            ins = nc.scalar.activation(raw[:, r % 2, :], ps[:, b, 0:T], ACT.Copy)
                        ins.then_inc(L.sem("act_took"), 1)
                    L.end_stage(act, 2)

                    act.wait_ge(L.sem("gate_variance"), 1)
                    nc.scalar.activation(small[:, 20:22], small[:, 16:18], ACT.Sqrt).then_inc(L.sem("gate_root"), 1)
                    for h in range(8):
                        act.wait_ge(L.sem("logits_ready"), h + 1)
                        if h >= 4:
                            act.wait_ge(L.sem("scored"), 2 * (h - 4) + 2)
                        nc.scalar.activation(relu[:, h % 4, :], ps[:, h % 4, 0:PACK], ACT.Relu
                                             ).then_inc(L.sem("logits_taken"), 1)
                    for u in range(2):
                        soft_act(act, L, u)
                    L.end_stage(act, 3)

                    for j in range(DK):
                        for q in range(2):
                            act.wait_ge(L.sem("tiles_done"), tb[MERGE] + 4 * j + 2 * q + 1)
                            if j >= 2:
                                act.wait_ge(L.sem("dve_took"), merge_v + 2 * j - 3 + q)
                            nc.scalar.activation(sig[:, 2 * (j % 2) + q, :], ps[:, 4 * (j % 2) + 2 * q, 0:T],
                                                 ACT.Sigmoid, bias=p1("b_gate")[:, DK * q + j:DK * q + j + 1]
                                                 ).then_inc(L.sem("act_took"), 1)
                    L.end_stage(act, 4)

                    norm_act(act, L, "ffn2")
                    ffn_act(act, L, tb[FFN2], ffn2_v)
                    L.end_stage(act, 5)

                @block.vector
                def _(dve):
                    chain = Chain(dve, L.sem("dve_chain"))
                    dve.wait_ge(L.sem("params_landed"), 16)
                    norm_dve(dve, L, chain, "ffn1", p1("g_ffn1"), hT)
                    ffn_dve(dve, L, 0, 0)
                    L.end_stage(dve, 1)

                    norm_dve(dve, L, chain, "mix", p1("g_mix"), hT)
                    for r, i in enumerate(ropes):
                        kind, n = TILES[i]
                        rope_dve(dve, L, chain, r, proj_a + i + 1, P, const("cos64"), const("sin64"),
                                 rot[:, ROT[kind] + n, :])
                    L.end_stage(dve, 2)

                    for c in range(TT):
                        chain.link(nc.vector.bn_stats(small[:, 6 * c:6 * c + 6], va_tok[:, c, :]))
                        chain.link(nc.vector.bn_aggr(small[:, 12 + 2 * c:14 + 2 * c], small[:, 6 * c:6 * c + 6]))
                        ins = nc.vector.tensor_scalar(small[:, 16 + c:17 + c], small[:, 13 + 2 * c:14 + 2 * c],
                                                      EPS, None, ALU.add)
                        if c == 0:
                            chain.link(ins)
                    ins.then_inc(L.sem("gate_variance"), 1)
                    ws = p1("w_s").rearrange("p (g t) -> p g t", g=4)
                    chain.link(nc.vector.tensor_tensor(
                        ws, ws, const("upto").rearrange("p (o t) -> p o t", o=1).to_broadcast([P, 4, P]), ALU.mult))
                    dve.wait_ge(L.sem("gate_root"), 1)
                    chain.link(nc.vector.reciprocal(small[:, 18:20], small[:, 20:22]))
                    for c in range(TT):
                        v = va_tok[:, c, :]
                        chain.link(nc.vector.tensor_scalar(v, v, small[:, 12 + 2 * c:13 + 2 * c],
                                                           small[:, 18 + c:19 + c], ALU.subtract, ALU.mult))
                        chain.link(nc.vector.tensor_tensor(v, v, p1("ln_g"), ALU.mult))
                        nc.vector.tensor_tensor(v, v, p1("ln_b"), ALU.add).then_inc(L.sem("gate_normed"), 1)
                    for h in range(8):
                        dve.wait_ge(L.sem("logits_taken"), h + 1)
                        for t, (a, b) in enumerate(HALVES):
                            if h:
                                dve.wait_ge(L.sem("scored"), 2 * (h - 1) + t + 1)
                            nc.vector.scalar_tensor_tensor(
                                score[:, a:b], relu[:, h % 4, a:b], wi_tok[:, t, h:h + 1],
                                (score if h else const("causal"))[:, a:b], ALU.mult, ALU.add
                            ).then_inc(L.sem("scored"), 1)
                    dve.wait_ge(L.sem("tokens_mixed"), 1)
                    bs = p1("b_s").rearrange("p (g t) -> p g t", g=4)
                    chain.link(nc.vector.tensor_tensor(ybT[:, :, 0:P], ps[:, 4:8, 0:P], bs, ALU.add))
                    nc.vector.tensor_tensor(ybT[:, :, P:T], ps[:, 4:8, P:T], bs, ALU.add
                                            ).then_inc(L.sem("tokens_taken"), 1)
                    dve.wait_ge(L.sem("tokens_taken"), 1)
                    chain.link(nc.vector.tensor_tensor(yaT[:, :, :], ybT[:, :, :], uT[:, :, :], ALU.mult))
                    dve.wait_ge(L.sem("scored"), 16)
                    for a, b in HALVES:
                        for _ in range(TOPK // 8):
                            chain.link(nc.vector.max(top8[:, :], score[:, a:b]))
                            chain.link(nc.vector.match_replace(score[:, a:b], top8[:, :], score[:, a:b], TAKEN))
                    chain.link(nc.vector.tensor_scalar(keyset[:, :], score[:, :], 0.5 * TAKEN, NEG,
                                                       ALU.is_gt, ALU.mult))
                    chain.link(nc.vector.tensor_tensor(keyset[:, :], keyset[:, :], const("causal"), ALU.add))
                    bias = keyset[:, :].rearrange("p (o n) -> p o n", o=1).to_broadcast([P, 4, PACK])
                    for u in range(2):
                        soft_dve(dve, L, chain, u, HD ** -0.5, bias)
                        dve.wait_ge(L.sem("mixed"), u + 1)
                        nc.vector.tensor_copy(ybT[:, 2 * u:2 * u + 2, :], ps[:, 4:6, 0:T]
                                              ).then_inc(L.sem("mixed_taken"), 1)
                    L.end_stage(dve, 3)

                    for j in range(DK):
                        for q in range(2):
                            dve.wait_ge(L.sem("tiles_done"), tb[MERGE] + 4 * j + 2 * q + 2)
                            dve.wait_ge(L.sem("act_took"), merge_a + 2 * j + q + 1)
                            nc.vector.tensor_tensor(gated[:, 2 * (j % 2) + q, :], sig[:, 2 * (j % 2) + q, :],
                                                    ps[:, 4 * (j % 2) + 2 * q + 1, 0:T], ALU.mult
                                                    ).then_inc(L.sem("dve_took"), 1)
                        dve.wait_ge(L.sem("dve_took"), merge_v + 2 * j + 2)
                        nc.vector.tensor_tensor(zT[:, j, :], gated[:, 2 * (j % 2), :], gated[:, 2 * (j % 2) + 1, :],
                                                ALU.add).then_inc(L.sem("z_ready"), 1)
                    out_dve(dve, L, tb[OUT])
                    L.end_stage(dve, 4)

                    norm_dve(dve, L, chain, "ffn2", p1("g_ffn2"), hT)
                    ffn_dve(dve, L, tb[FFN2], ffn2_a)
                    L.end_stage(dve, 5)
            return L

        def second_layer(l):
            with ExitStack() as stack:
                L = Layer(stack, STEPS2, [4] * 8 + [10, 4] + [8] * 8 + [4, 4], w2_in, par2, par2_in, l)
                tb = L.tiles_before
                MERGE, OUT = 10, 18
                TILES = []

                def put(step, kind, count, c0, width):
                    for n in range(count):
                        TILES.append((kind, n, step, c0 + (0 if kind in TOKEN else n * width), width))

                TOKEN = ("a_v", "c_vg", "d_v", "b_v")
                put(0, "a_qk", 4, 0, P)
                put(1, "a_v", 2, 0, BW), put(1, "a_gate", 2, BW, P)
                put(2, "cq", 1, 0, P), put(2, "cq_rest", 1, P, HD), put(2, "ckv", 1, 192, P), put(2, "kpe", 1, BW, 96)
                put(3, "bc_gate", 4, 0, P)
                put(4, "c_qk", 4, 0, P)
                put(5, "c_cmp", 2, 0, P), put(5, "c_vg", 2, BW, 140)
                put(6, "d_qk", 4, 0, P)
                put(7, "d_v", 2, 0, BW), put(7, "d_gate", 2, BW, P)
                put(8, "b_q", 4, 0, 96), put(8, "b_k", 4, 768, HD), put(8, "b_v", 2, 1024, BW)
                put(9, "hidden", 2, 0, P), put(9, "k_cmp", 1, 0, P), put(9, "v_cmp", 1, 0, HD)
                WIDTH = [512, 512, 352, 512, 512, C2_COLS, 512, 512]
                where = {(kind, n): i for i, (kind, n, *_) in enumerate(TILES)}
                took = lambda kind, n=0: where[kind, n] + 1
                ropes = [where["kpe", 0]] + [where["b_q", h] for h in range(4)]
                merge_a, merge_v = len(TILES), 0
                out_v = merge_v + 32
                scale_b = 96 ** -0.5

                def half(src, h):
                    return src[HD * (h % 2):HD * (h % 2) + HD, h // 2, :]

                def twice(src, h):
                    return src[HD * (h % 2):HD * (h % 2) + HD, :]

                block = stack.enter_context(nc.Block())

                @block.sync
                def _(sp):
                    stream(sp, L)

                @block.tensor
                def _(pe):
                    pe.wait_ge(L.sem("params_landed"), 16)
                    norm_pe(pe, L, "mix")
                    pe.wait_ge(L.sem("normed_mix"), DK)
                    h_ = lambda k: hT[:, k, :]
                    for i, (kind, n, step, c0, w) in enumerate(TILES):
                        b, slot = i % 6, step % 2
                        if i in tb:
                            L.landed(pe, step)
                        if i >= 6:
                            pe.wait_ge(L.sem("act_took"), i - 5)
                        if kind == "b_q":
                            pe.wait_ge(L.sem("latents_normed"), 3)
                            mm = product(ps[0:96, b, 0:T], slot, 0, 384, c0, w, lambda k: cqT[:, k, :], 2,
                                         rows=(P, HD))
                        elif kind == "b_k":
                            mm = product(ps[0:HD, b, 0:T], slot, 0, 0, c0, w, lambda k: ckvT, 1)
                        elif kind == "b_v":
                            mm = product_tok(ps[:, b, 0:BW], slot, 0, 0, c0, BW, lambda k: ckvT[:, n * P:n * P + P], 1)
                        elif kind == "hidden":
                            pe.wait_ge(L.sem("act_took"), took("c_cmp", 1))
                            for k in range(16):
                                nc.tensor.matmul(ps[:, b, 0:NCMP], ring[:, slot, (16 * n + k) * P:(16 * n + k + 1) * P],
                                                 cmpT[:, n, 2 * k:2 * k + 16 * (NCMP - 1) + 1:16],
                                                 start=(k == 0), stop=(k == 15))
                            for k in range(16):
                                mm = nc.tensor.matmul(ps[:, b, 16:17], ring[:, slot, (16 * n + k) * P:(16 * n + k + 1) * P],
                                                      p2("pos")[:, 16 * n + k:16 * n + k + 1],
                                                      start=(k == 0), stop=(k == 15))
                        elif kind == "k_cmp":
                            pe.wait_ge(L.sem("act_took"), took("hidden", 0))
                            mm = nc.tensor.matmul(ps[:, b, 0:NCMP], ring[:, slot, 4096:4096 + P], cmp_hidden[:, 0, :],
                                                  start=True, stop=True)
                        elif kind == "v_cmp":
                            pe.wait_ge(L.sem("act_took"), took("hidden", 1))
                            mm = nc.tensor.matmul(ps[0:NCMP, b, 0:HD], cmp_hidden[:, 1, :],
                                                  ring[:, slot, 4096 + P:4096 + P + HD], start=True, stop=True)
                        elif kind in TOKEN:
                            mm = product_tok(ps[:, b, 0:w], slot, 0, WIDTH[step], c0, w,
                                             lambda k: hT[:, k, n * P:n * P + P], DK)
                        else:
                            mm = product(ps[0:w, b, 0:T], slot, 0, WIDTH[step], c0, w, h_, DK)
                        mm.then_inc(L.sem("tiles_done"), 1)
                        if i - 1 in ropes:
                            rope_pe(pe, L, ropes.index(i - 1), i, 96, con[0:96, CONST["swap96"][0]:CONST["swap96"][1]])
                        if kind == "bc_gate" and n == 1:
                            pe.wait_ge(L.sem("latents_squared"), 3)
                            nc.tensor.matmul(ps[:, 7, 0:T], ones[:, :], latent_sq[:, 0, :], start=True, stop=False)
                            nc.tensor.matmul(ps[:, 7, 0:T], ones[0:HD, :], latent_sq[0:HD, 1, :], start=False, stop=True)
                            nc.tensor.matmul(ps[:, 7, T:2 * T], ones[:, :], latent_sq[:, 2, :], start=True, stop=True
                                             ).then_inc(L.sem("latents_summed"), 1)
                    L.end_stage(pe, 1)

                    units = (
                        (lambda h: half(a_qkT, h), lambda h: half(a_qkT[:, 2:4, :], h),
                         lambda t, h: a_v[:, t, h * HD:h * HD + HD]),
                        (lambda h: b_qT[0:96, h, :], lambda h: b_kT[0:96, h, :],
                         lambda t, h: b_v[:, t, h * HD:h * HD + HD]),
                        (lambda h: half(c_qkT, h), lambda h: twice(c_qkT[:, 2, :], h), lambda t, h: c_vg[:, t, 0:HD]),
                        (lambda h: half(c_qkT, h), lambda h: twice(c_qkT[:, 3, :], h), lambda t, h: c_vg[:, t, HD:P]))
                    for u, (q, k, v) in enumerate(units):
                        scores_pe(pe, L, u, q, k)
                        mix_pe(pe, L, u, v)

                    pe.wait_ge(L.sem("scores_taken"), 4)
                    for h in range(4):
                        for t in range(TT):
                            a = (h // 2 * TT + t) * NCMP
                            mm = nc.tensor.matmul(ps[:, h % 2, a:a + NCMP], half(c_qkT, h)[:, t * P:t * P + P],
                                                  twice(k_cmpT, h), start=True, stop=True)
                    mm.then_inc(L.sem("cmp_scores"), 1)
                    pe.wait_ge(L.sem("cmp_probs"), 1)
                    for h in range(4):
                        for t in range(TT):
                            a = (h * TT + t) * NCMP
                            mm = nc.tensor.transpose(ps[0:NCMP, 2 + h // 2, (h % 2 * TT + t) * P:(h % 2 * TT + t + 1) * P],
                                                     cmp_p[:, a:a + NCMP], const("ident"))
                    mm.then_inc(L.sem("cmp_turned"), 1)
                    pe.wait_ge(L.sem("cmp_copied"), 1)
                    pe.wait_ge(L.sem("mixed_taken"), 4)
                    for h in range(4):
                        o = HD * (h % 2)
                        mm = nc.tensor.matmul(ps[o:o + HD, 4 + h // 2, 0:T], v_cmp[0:NCMP, :], cmp_pT[0:NCMP, h, :],
                                              start=True, stop=True)
                    mm.then_inc(L.sem("cmp_mixed"), 1)

                    for h in range(4):
                        q, k = half(d_qkT, h), half(d_qkT[:, 2:4, :], h)
                        nc.tensor.matmul(ps[:, h, 0:T], k[:, 0:P], q, start=True, stop=True)
                        mm = nc.tensor.matmul(ps[:, h, T:PACK], k[:, P:T], q[:, P:T], start=True, stop=True)
                    mm.then_inc(L.sem("stick_scores"), 1)
                    pe.wait_ge(L.sem("stick_logs"), 1)
                    pe.wait_ge(L.sem("cmp_taken"), 1)
                    for h in range(4):
                        s = stick_log[:, h, :]
                        nc.tensor.matmul(ps[:, 4 + h, T:PACK], const("later"), s[:, T:PACK], start=True, stop=True)
                        nc.tensor.matmul(ps[:, 4 + h, 0:T], const("later"), s[:, 0:T], start=True, stop=False)
                        mm = nc.tensor.matmul(ps[:, 4 + h, P:T], ones[:, :], s[:, T:PACK], start=False, stop=True)
                    mm.then_inc(L.sem("stick_sums"), 1)
                    pe.wait_ge(L.sem("stick_probs"), 1)
                    mix_values(lambda t, h: d_v[:, t, h * HD:h * HD + HD]).then_inc(L.sem("stick_mixed"), 1)
                    L.end_stage(pe, 2)

                    def merge_step(c, pair, first=False):
                        L.landed(pe, MERGE + pair, c)
                        for q in range(4):
                            nt, br = q // 2, q % 2
                            for o, (kt, src, sem, base) in enumerate((
                                    (DK, hT, "act_took", merge_a), (2, yT[2 * pair + br], "dve_took", merge_v))):
                                if not first:
                                    pe.wait_ge(L.sem(sem), base + 4 * (2 * c + pair) + q - 3)
                                product(ps[:, 2 * q + o, 0:T], pair, (10 * br + DK * o) * 256, 256, nt * P, P,
                                        lambda k: src[:, k, :], kt).then_inc(L.sem("tiles_done"), 1)

                    merge_step(0, 0, first=True)
                    merge_step(0, 1)
                    with pe.Fori(1, 4) as c:
                        merge_step(c, 0)
                        merge_step(c, 1)
                    pe.wait_ge(L.sem("z_added"), 24)
                    out_pe(pe, L, OUT, out_v)
                    L.end_stage(pe, 3)

                @block.scalar
                def _(act):
                    norm_act(act, L, "mix")
                    own = Chain(act, L.sem("act_chain"))
                    for i, (kind, n, step, c0, w) in enumerate(TILES):
                        act.wait_ge(L.sem("tiles_done"), i + 1)
                        src = ps[0:min(w, P), i % 6, 0:T]
                        if kind in ("cq", "cq_rest", "ckv"):
                            j = ("cq", "cq_rest", "ckv").index(kind)
                            nc.scalar.activation(latent_sq[0:w, j, :], src, ACT.Square
                                                 ).then_inc(L.sem("latents_squared"), 1)
                            dst, f = (ckvT if j == 2 else cqT[0:w, j, :]), ACT.Copy
                        elif kind == "a_qk":
                            dst, f = a_qkT[:, n, :], ACT.Copy
                        elif kind == "c_qk":
                            dst, f = c_qkT[:, n, :], ACT.Copy
                        elif kind == "d_qk":
                            dst, f = d_qkT[:, n, :], ACT.Copy
                        elif kind == "a_gate":
                            dst, f = gateT[0][:, n, :], ACT.Silu
                        elif kind == "bc_gate":
                            dst, f = gateT[1 + n // 2][:, n % 2, :], ACT.Silu
                        elif kind == "d_gate":
                            dst, f = gateT[3][:, n, :], ACT.Silu
                        elif kind == "b_k":
                            dst, f = b_kT[0:HD, n, :], ACT.Copy
                        elif kind in ("a_v", "b_v", "d_v"):
                            dst, f = {"a_v": a_v, "b_v": b_v, "d_v": d_v}[kind][:, n, :], ACT.Copy
                            src = ps[:, i % 6, 0:BW]
                        elif kind == "c_vg":
                            own.link(nc.scalar.activation(c_g[:, n, :], ps[:, i % 6, P:140], ACT.Sigmoid))
                            dst, f, src = c_vg[:, n, :], ACT.Copy, ps[:, i % 6, 0:P]
                        elif kind == "c_cmp":
                            own.link(nc.scalar.activation(cmpT[0:HD, n, :], ps[0:HD, i % 6, 0:T], ACT.Copy))
                            dst, f, src = cmpT[HD:P, n, 0:T - 1], ACT.Copy, ps[HD:P, i % 6, 1:T]
                        elif kind == "hidden":
                            act.wait_ge(L.sem("cmp_bias"), n + 1)
                            nc.scalar.activation(cmp_hidden[:, n, :], ps[:, i % 6, 0:NCMP], ACT.Gelu_apprx_tanh,
                                                 bias=cmp_b[:, n:n + 1]).then_inc(L.sem("act_took"), 1)
                            continue
                        elif kind == "k_cmp":
                            nc.scalar.activation(k_cmpT, ps[:, i % 6, 0:NCMP], ACT.Identity, bias=p2("b2_k")
                                                 ).then_inc(L.sem("act_took"), 1)
                            continue
                        elif kind == "v_cmp":
                            dst, f, src = v_cmp[0:NCMP, :], ACT.Copy, ps[0:NCMP, i % 6, 0:HD]
                        else:
                            r = ropes.index(i)
                            if r >= 2:
                                act.wait_ge(L.sem("turned_taken"), r - 1)
                            dst, f = raw[0:96, r % 2, :], ACT.Copy
                        nc.scalar.activation(dst, src, f).then_inc(L.sem("act_took"), 1)
                        if kind == "bc_gate" and n == 3:
                            act.wait_ge(L.sem("latents_mean"), 1)
                            nc.scalar.activation(latent_sq[:, 0:2, :], latent_r, ACT.Sqrt
                                                 ).then_inc(L.sem("latents_root"), 1)
                    L.end_stage(act, 1)

                    for u in range(4):
                        soft_act(act, L, u)
                    act.wait_ge(L.sem("cmp_shifted"), 1)
                    nc.scalar.activation(cmp_p, cmp_p, ACT.Exp).then_inc(L.sem("cmp_exps"), 1)
                    act.wait_ge(L.sem("cmp_turned"), 1)
                    nc.scalar.activation(cmp_pT[0:NCMP, :, :].rearrange("p (b h) t -> p b (h t)", b=2),
                                         ps[0:NCMP, 2:4, :], ACT.Copy).then_inc(L.sem("cmp_copied"), 1)
                    act.wait_ge(L.sem("stick_scores"), 1)
                    nc.scalar.activation(stick_a, ps[:, 0:4, 0:PACK], ACT.Abs, scale=HD ** -0.5
                                         ).then_inc(L.sem("stick_abs"), 1)
                    act.wait_ge(L.sem("stick_abs"), 1)
                    own.link(nc.scalar.activation(stick_a, stick_a, ACT.Exp, scale=-1.0))
                    nc.scalar.activation(stick_a, stick_a, ACT.Ln, bias=1.0).then_inc(L.sem("stick_log1p"), 1)
                    act.wait_ge(L.sem("stick_exponent"), 1)
                    nc.scalar.activation(probsT, stick_a, ACT.Exp).then_inc(L.sem("stick_exps"), 1)
                    L.end_stage(act, 2)

                    for s in range(8):
                        for q in range(4):
                            br, n = 2 * (s % 2) + q % 2, 2 * (s // 2) + q // 2
                            act.wait_ge(L.sem("tiles_done"), tb[MERGE] + 8 * s + 2 * q + 1)
                            if s:
                                act.wait_ge(L.sem("dve_took"), merge_v + 4 * s + q - 3)
                            nc.scalar.activation(sig[:, q, :], ps[:, 2 * q, 0:T], ACT.Sigmoid,
                                                 bias=p2("b_merge")[:, DK * br + n:DK * br + n + 1]
                                                 ).then_inc(L.sem("act_took"), 1)
                    L.end_stage(act, 3)

                @block.vector
                def _(dve):
                    chain = Chain(dve, L.sem("dve_chain"))
                    dve.wait_ge(L.sem("params_landed"), 16)
                    norm_dve(dve, L, chain, "mix", p2("g_norm"), hT)
                    c96, s96 = (con[0:96, CONST[n][0]:CONST[n][1]] for n in ("cos96", "sin96"))
                    rope_dve(dve, L, chain, 0, took("kpe"), 96, c96, s96, kpeT[0:96, :])
                    chain.link(nc.vector.tensor_copy(
                        b_kT[HD:96, :, :], kpeT[HD:96, :].rearrange("p (o t) -> p o t", o=1).to_broadcast([32, 4, T])))
                    dve.wait_ge(L.sem("latents_summed"), 1)
                    chain.link(nc.vector.tensor_scalar(latent_r[:, 0, :], ps[:, 7, 0:T], 1.0 / 192, EPS, ALU.mult, ALU.add))
                    nc.vector.tensor_scalar(latent_r[:, 1, :], ps[:, 7, T:2 * T], 1.0 / P, EPS, ALU.mult, ALU.add
                                            ).then_inc(L.sem("latents_mean"), 1)
                    dve.wait_ge(L.sem("latents_root"), 1)
                    chain.link(nc.vector.reciprocal(latent_r, latent_sq[:, 0:2, :]))
                    for j, (v, w, g) in enumerate(((cqT[:, 0, :], P, p2("g_q")[:, 0:1]),
                                                   (cqT[0:HD, 1, :], HD, p2("g_q")[0:HD, 1:2]), (ckvT, P, p2("g_kv")))):
                        nc.vector.scalar_tensor_tensor(v, v, g, latent_r[0:w, j // 2, :], ALU.mult, ALU.mult
                                                       ).then_inc(L.sem("latents_normed"), 1)
                    for h in range(4):
                        rope_dve(dve, L, chain, 1 + h, took("b_q", h), 96, c96, s96, b_qT[0:96, h, :])
                    for n in range(2):
                        dve.wait_ge(L.sem("tiles_done"), took("hidden", n))
                        nc.vector.tensor_tensor(cmp_b[:, n:n + 1], ps[:, where["hidden", n] % 6, 16:17],
                                                p2("b1")[:, n:n + 1], ALU.add).then_inc(L.sem("cmp_bias"), 1)
                    dve.wait_ge(L.sem("act_took"), took("v_cmp"))
                    chain.link(nc.vector.tensor_tensor(v_cmp[0:NCMP, :], v_cmp[0:NCMP, :], p2("b2_v")[0:NCMP, :], ALU.add))
                    L.end_stage(dve, 1)

                    causal = const("causal").rearrange("p (o n) -> p o n", o=1).to_broadcast([P, 4, PACK])
                    gates = lambda b: c_g[:, :, b::3]
                    for u, (scale, bias, gate) in enumerate((
                            (HD ** -0.5, const("alibi_a", 4), None), (scale_b, causal, None),
                            (HD ** -0.5, const("alibi_c", 4), gates(1)), (HD ** -0.5, const("alibi_c", 4), gates(2)))):
                        soft_dve(dve, L, chain, u, scale, bias, gate)
                        dve.wait_ge(L.sem("mixed"), u + 1)
                        if u < 2:
                            ins = nc.vector.tensor_tensor(yT[u], ps[:, 4:6, 0:T], gateT[u], ALU.mult)
                        elif u == 2:
                            ins = nc.vector.tensor_copy(yT[2], ps[:, 4:6, 0:T])
                        else:
                            ins = nc.vector.tensor_tensor(yT[2], ps[:, 4:6, 0:T], yT[2], ALU.add)
                        ins.then_inc(L.sem("mixed_taken"), 1)
                        dve.wait_ge(L.sem("mixed_taken"), u + 1)

                    dve.wait_ge(L.sem("cmp_scores"), 1)
                    cp = cmp_p.rearrange("p (h n) -> p h n", h=4)
                    al = const("alibi_cmp", 4)
                    for odd in range(2):
                        chain.link(nc.vector.scalar_tensor_tensor(
                            cp[:, odd::2, :], ps[:, odd, 0:4 * NCMP].rearrange("p (h n) -> p h n", h=2), HD ** -0.5,
                            al[:, odd::2, :], ALU.mult, ALU.add))
                    c8 = cmp_p.rearrange("p (g n) -> p g n", g=8)
                    wide = lambda v: v.rearrange("p (g o) -> p g o", o=1).to_broadcast([P, 8, NCMP])
                    chain.link(nc.vector.reduce_max(cmp_m, c8, AX.X, negate=True))
                    chain.link(nc.vector.tensor_scalar(cmp_m, cmp_m, -0.1 * NEG, None, ALU.min))
                    nc.vector.tensor_tensor(c8, c8, wide(cmp_m), ALU.add).then_inc(L.sem("cmp_shifted"), 1)
                    dve.wait_ge(L.sem("cmp_exps"), 1)
                    chain.link(nc.vector.reduce_sum(cmp_m, c8, AX.X))
                    chain.link(nc.vector.tensor_scalar(cmp_m, cmp_m, 1e-30, None, ALU.max))
                    chain.link(nc.vector.reciprocal(cmp_m, cmp_m))
                    chain.link(nc.vector.tensor_tensor(cmp_m.rearrange("p (h t) -> p h t", h=4),
                                                       cmp_m.rearrange("p (h t) -> p h t", h=4),
                                                       gates(0).rearrange("p t h -> p h t"), ALU.mult))
                    nc.vector.tensor_tensor(c8, c8, wide(cmp_m), ALU.mult).then_inc(L.sem("cmp_probs"), 1)
                    dve.wait_ge(L.sem("cmp_mixed"), 1)
                    nc.vector.tensor_tensor(yT[2], ps[:, 4:6, 0:T], yT[2], ALU.add).then_inc(L.sem("cmp_taken"), 1)
                    dve.wait_ge(L.sem("cmp_taken"), 1)
                    chain.link(nc.vector.tensor_tensor(yT[2], yT[2], gateT[2], ALU.mult))

                    before = const("before").rearrange("p (o n) -> p o n", o=1).to_broadcast([P, 4, PACK])
                    dve.wait_ge(L.sem("stick_abs"), 1)
                    chain.link(nc.vector.tensor_scalar(stick_b, ps[:, 0:4, 0:PACK], HD ** -0.5, 0.0, ALU.mult, ALU.max))
                    dve.wait_ge(L.sem("stick_log1p"), 1)
                    chain.link(nc.vector.tensor_tensor(stick_b, stick_b, stick_a, ALU.add))
                    nc.vector.tensor_tensor(stick_log, stick_b, before, ALU.mult).then_inc(L.sem("stick_logs"), 1)
                    chain.link(nc.vector.scalar_tensor_tensor(stick_a, ps[:, 0:4, 0:PACK], HD ** -0.5, stick_b,
                                                              ALU.mult, ALU.subtract))
                    dve.wait_ge(L.sem("stick_sums"), 1)
                    nc.vector.tensor_tensor(stick_a, stick_a, ps[:, 4:8, 0:PACK], ALU.subtract
                                            ).then_inc(L.sem("stick_exponent"), 1)
                    dve.wait_ge(L.sem("stick_exps"), 1)
                    nc.vector.tensor_tensor(probsT, probsT, before, ALU.mult).then_inc(L.sem("stick_probs"), 1)
                    dve.wait_ge(L.sem("stick_mixed"), 1)
                    nc.vector.tensor_tensor(yT[3], ps[:, 4:6, 0:T], gateT[3], ALU.mult)
                    L.end_stage(dve, 2)

                    added = 0
                    for s in range(8):
                        for q in range(4):
                            n = 2 * (s // 2) + q // 2
                            start = s % 2 == 0 and q % 2 == 0
                            dve.wait_ge(L.sem("tiles_done"), tb[MERGE] + 8 * s + 2 * q + 2)
                            dve.wait_ge(L.sem("act_took"), merge_a + 4 * s + q + 1)
                            nc.vector.tensor_tensor(zT[:, n, :] if start else gated[:, q, :], sig[:, q, :],
                                                    ps[:, 2 * q + 1, 0:T], ALU.mult).then_inc(L.sem("dve_took"), 1)
                            dve.wait_ge(L.sem("dve_took"), merge_v + 4 * s + q + 1)
                            if not start:
                                if added:
                                    dve.wait_ge(L.sem("z_added"), added)
                                nc.vector.tensor_tensor(zT[:, n, :], zT[:, n, :], gated[:, q, :], ALU.add
                                                        ).then_inc(L.sem("z_added"), 1)
                                added += 1
                    out_dve(dve, L, tb[OUT])
                    L.end_stage(dve, 3)
            return L


        def final_norm(name, gain, to_dram):
            with ExitStack() as stack:
                L = Layer(stack, [0], [0], None, None, None, None)
                block = stack.enter_context(nc.Block())

                @block.tensor
                def _(pe):
                    norm_pe(pe, L, name)

                @block.scalar
                def _(act):
                    norm_act(act, L, name)

                @block.vector
                def _(dve):
                    norm_dve(dve, L, Chain(dve, L.sem("dve_chain")), name, gain, hT if to_dram else xT)

                if to_dram:
                    @block.sync
                    def _(sp):
                        sp.wait_ge(L.sem("normed_" + name), DK)
                        sp.dma_start(out, hT[:, :, :]).then_inc(L.sem("out_written"), 16)
                        sp.wait_ge(L.sem("out_written"), 16)
            L.clear()

        def final(name):
            a, b = FIN[name]
            return fin[:, a:b]

        with nc.Fori(0, DEPTH) as l:
            first_layer(l).clear()
        final_norm("final1", final("final1"), False)
        with nc.Fori(0, DEPTH) as l:
            second_layer(l).clear()
        final_norm("final2", final("final2"), True)


def rope_tables(half, pad, total):
    if half == HD // 2:
        inv = np.float32(10000.0) ** (-np.arange(0, 2 * half, 2, dtype=np.float32) / np.float32(2 * half))
    else:
        inv = np.float32(10000.0) ** (-np.arange(half, dtype=np.float32) / np.float32(half))
    ang = np.arange(T, dtype=np.float32)[:, None] * inv.astype(np.float32)[None, :]
    c, s = np.cos(ang).T, np.sin(ang).T
    cos = np.concatenate([np.ones((pad, T)), c, c])
    sin = np.concatenate([np.zeros((pad, T)), -s, s])
    swap = np.zeros((pad + 2 * half, pad + 2 * half))
    i = np.arange(half)
    swap[pad + i, pad + half + i] = swap[pad + half + i, pad + i] = 1
    n = total // (pad + 2 * half)
    return np.tile(cos, (n, 1)), np.tile(sin, (n, 1)), np.kron(np.eye(n), swap)


def constants():
    c = np.zeros((P, NCONST), np.float32)

    def put(name, v):
        a, b = CONST[name]
        v = np.asarray(v, np.float32)
        c[:v.shape[0], a:b] = v.reshape(v.shape[0], -1)

    put("ident", np.eye(P))
    cos, sin, swap = rope_tables(32, 0, P)
    put("cos64", cos), put("sin64", sin), put("swap64", swap)
    cos, sin, swap = rope_tables(16, 64, 96)
    put("cos96", cos), put("sin96", sin), put("swap96", swap)
    t, s = np.arange(T)[:, None], np.arange(T)[None, :]

    def pack(m):
        return np.concatenate([m[:P, :P], m[P:, :]], axis=1)

    dist = t - s
    put("causal", pack(np.where(dist >= 0, 0.0, NEG)))
    slopes = 2.0 ** -(np.arange(8) + 1.0)
    patterns = sum(((dist >= 0) & (dist <= w) & (dist % d == 0)).astype(int) for w, d in ((128, 1), (512, 4), (2048, 16)))
    log_n = np.where(patterns > 0, np.log(np.maximum(patterns, 1)), NEG)
    put("alibi_a", np.stack([pack(np.where(patterns > 0, log_n - m * dist, NEG)) for m in slopes[0::2]], 1))
    put("alibi_c", np.stack([pack(np.where(dist >= 0, -m * dist, NEG)) for m in slopes[1::2]], 1))
    far = t - (16 * np.arange(NCMP) + 31)[None, :]
    cmp_ = np.stack([np.where(far >= 0, -m * far, NEG) for m in slopes[1::2]], 1)
    put("alibi_cmp", cmp_.reshape(TT, P, 4, NCMP).transpose(1, 2, 0, 3))
    put("upto", np.arange(P)[:, None] <= np.arange(P)[None, :])
    strict = (np.arange(P)[:, None] < np.arange(P)[None, :]).astype(np.float32)
    put("before", np.concatenate([strict, np.ones((P, P)), strict], axis=1))
    put("later", np.arange(P)[:, None] > np.arange(P)[None, :])
    return c


def tiles(w):
    k, c = w.shape
    return w.reshape(k // P, P, c).transpose(1, 0, 2).reshape(P, -1)


def vec(v):
    return v.reshape(-1, P).T


def rows(v):
    return np.broadcast_to(v.reshape(1, -1), (P, v.size))


def lay_out_first(a, l):
    def ffn(gu, down):
        out = []
        for i in range(FF // 256):
            c = slice(256 * i, 256 * i + 256)
            out.append(tiles(np.concatenate([gu[:, :FF][:, c], gu[:, FF:][:, c]], axis=1)))
        return out + [tiles(down[:, 256 * i:256 * i + 256]) for i in range(4)]

    w = a["w_in"][l]
    u, va, q, k, v = (w[:, 512 * i:512 * i + 512] for i in range(5))
    qi, ki, wi, ga, gb = (w[:, x:y] for x, y in ((2560, 3072), (3072, 3136), (3136, 3144), (3144, 4168), (4168, 5192)))
    steps = ffn(a["ffn1_w_gu"][l], a["ffn1_w_down"][l])
    steps += [tiles(x) for x in (u, va, q, k, qi, v, np.concatenate([ki, ki], 1), wi)]
    for i in range(4):
        c = slice(256 * i, 256 * i + 256)
        steps.append(np.concatenate([tiles(x[:, c]) for x in (ga, gb, a["w_pa"][l], a["w_pb"][l])], axis=1))
    steps += [tiles(a["w_out"][l][:, 512 * i:512 * i + 512]) for i in range(2)]
    steps += ffn(a["ffn2_w_gu"][l], a["ffn2_w_down"][l])
    assert [s.shape[1] for s in steps] == STEPS1
    par = np.concatenate([vec(a["ffn1_norm"][l]), vec(a["mix_norm"][l]), vec(a["ffn2_norm"][l]), vec(a["b_gate"][l]),
                          rows(a["gmlp_ln_g"][l]), rows(a["gmlp_ln_b"][l]), rows(a["gmlp_b_s"][l]),
                          a["gmlp_w_s"][l].transpose(2, 0, 1).reshape(P, -1)], axis=1)
    return np.concatenate(steps, axis=1), par


def lay_out_second(a, l):
    a = {name[:-2]: v for name, v in a.items() if name.endswith("_2")}
    w, at, cols = a["w_in"][l], 0, {}
    for name, n in (("a_q", 256), ("a_k", 256), ("a_v", 256), ("a_gate", 256), ("b_cq", 192), ("b_ckv", 128),
                    ("b_kpe", 32), ("b_gate", 256), ("c_q", 256), ("kc", 64), ("vc", 64), ("ks", 64), ("vs", 64),
                    ("kw", 64), ("vw", 64), ("c_g", 12), ("c_gate", 256), ("d_q", 256), ("d_k", 256), ("d_v", 256),
                    ("d_gate", 256)):
        cols[name] = w[:, at:at + n]
        at += n
    assert at == w.shape[1]
    steps = [tiles(np.concatenate([cols[n] for n in names.split()], axis=1)) for names in (
        "a_q a_k", "a_v a_gate", "b_cq b_ckv b_kpe", "b_gate c_gate", "c_q ks ks kw kw", "kc kc vc vc vs vw c_g",
        "d_q d_k", "d_v d_gate")]
    uq = np.concatenate([a["mla_w_uq"][l], np.zeros((64, 384), np.float32)])
    ukv = a["mla_w_ukv"][l].reshape(P, 4, P)
    steps.append(np.concatenate([tiles(uq), ukv[:, :, :HD].reshape(P, -1), ukv[:, :, HD:].reshape(P, -1)], axis=1))
    w2 = a["nsa_w2"][l]
    steps.append(np.concatenate([tiles(a["nsa_w1"][l, 0]), tiles(a["nsa_w1"][l, 1]), w2[0], w2[0], w2[1],
                                 np.zeros((P, HD), np.float32)], axis=1))
    for c in range(4):
        cs = slice(256 * c, 256 * c + 256)
        for pair in range(2):
            steps.append(np.concatenate([tiles(v[:, cs]) for i in (2 * pair, 2 * pair + 1)
                                         for v in (a["w_merge"][l, i], a["w_branch"][l, i])], axis=1))
    steps += [tiles(a["w_out"][l][:, 512 * i:512 * i + 512]) for i in range(2)]
    assert [s.shape[1] for s in steps] == STEPS2, [s.shape[1] for s in steps]
    pad = np.zeros(64, np.float32)
    par = np.concatenate([vec(a["norm_g"][l]), vec(a["b_merge"][l].reshape(-1)),
                          vec(np.concatenate([a["mla_q_norm"][l], pad])), vec(a["mla_kv_norm"][l]),
                          a["nsa_b1"][l].T, vec(np.tile(a["nsa_b2"][l, 0], 2)),
                          a["nsa_pos"][l].reshape(32, P).T, rows(a["nsa_b2"][l, 1])], axis=1)
    return np.concatenate(steps, axis=1), par



def kernel(**inputs):
    import concourse.bacc as bacc
    from concourse.bass_utils import run_bass_kernel_spmd

    a = {name: np.asarray(v) for name, v in inputs.items()}
    w1, par1 = (np.ascontiguousarray(np.stack(v)) for v in zip(*(lay_out_first(a, l) for l in range(DEPTH))))
    w2, par2 = (np.ascontiguousarray(np.stack(v)) for v in zip(*(lay_out_second(a, l) for l in range(DEPTH))))
    arrays = {
        "x": np.ascontiguousarray(a["x"][0].T.reshape(DK, P, T).transpose(1, 0, 2)),
        "w1": w1, "w2": w2, "par1": par1, "par2": par2,
        "fin": np.concatenate([vec(a["final_norm"]), vec(a["final_norm_g_2"])], axis=1),
        "const": constants(),
    }
    arrays = {f"in_{name}": np.ascontiguousarray(v) for name, v in arrays.items()}
    nc = bacc.Bacc("TRN2", target_bir_lowering=False, num_devices=1)
    aps = [nc.dram_tensor(n, v.shape, F32, kind="ExternalInput").ap() for n, v in arrays.items()]
    out = nc.dram_tensor("out_0", [P, DK, T], F32, kind="ExternalOutput").ap()
    build(nc, *aps, out)
    r = run_bass_kernel_spmd(nc, [arrays], core_ids=[0])
    got = np.asarray(r.results[0]["out_0"])
    return got.transpose(1, 0, 2).reshape(D, T).T.reshape(1, T, D)
```

```python
from contextlib import ExitStack

import numpy as np

import concourse.bass as bass
from concourse import mybir

ALU = mybir.AluOpType
ACT = mybir.ActivationFunctionType
AX = mybir.AxisListType
F32 = mybir.dt.float32
F16 = mybir.dt.float16
BF16 = mybir.dt.bfloat16

P = 128
D = 1024
T = 256
TT = T // P
DEPTH = 2
DK = D // P
FF = 2816
FK = FF // P
EPS = 1e-6
NEG = -1e30
TAKEN = -3e38
PACK = 384
HD = 64
BW = 256
TOPK = 64
NCMP = 15

SLOTS = 4
FFN_STEPS, FFN_TILES = [DK * 256] * FK + [FK * P] * DK, [2] * FK + [1] * DK
PROJ1_STEPS, PROJ1_TILES = [DK * 256] * 12 + [DK * P, DK * 8], [2] * 12 + [1, 2]
MERGE1_STEPS, MERGE1_TILES = [24 * P] * DK, [4] * DK
OUT_STEPS, OUT_TILES = [DK * 256] * 4, [2] * 4
STEPS1 = FFN_STEPS + PROJ1_STEPS + MERGE1_STEPS + OUT_STEPS + FFN_STEPS
TILES1 = FFN_TILES + PROJ1_TILES + MERGE1_TILES + OUT_TILES + FFN_TILES
PROJ2_WIDTHS = [256] * 4 + [352] + [256] * 5 + [140] + [256] * 4
WHOLE2 = (15, 16, 17)
PROJ2_STEPS = [DK * w for w in PROJ2_WIDTHS] + [2 * 384 + 512, 16 * P, 16 * P + 256]
PROJ2_TILES = [2] * 4 + [4] + [2] * 10 + [10, 1, 3]
MERGE2_STEPS, MERGE2_TILES = [10 * 256] * 16, [4] * 16
STEPS2 = PROJ2_STEPS + MERGE2_STEPS + OUT_STEPS
TILES2 = PROJ2_TILES + MERGE2_TILES + OUT_TILES
SLOT = max(STEPS1 + STEPS2)
W1_TOTAL, W2_TOTAL = sum(STEPS1), sum(STEPS2)


def sections(widths):
    at, out = 0, {}
    for name, w in widths:
        out[name] = (at, at + w)
        at += w
    return out, at


CONST, NCONST = sections([
    ("ident", P), ("swap64", P), ("swap96", 96), ("cos64", T), ("sin64", T), ("cos96", T), ("sin96", T),
    ("causal", PACK), ("alibi_a", 4 * PACK), ("alibi_c", 4 * PACK), ("alibi_cmp", 4 * TT * NCMP),
    ("upto", P), ("before", PACK), ("later", P)])
PAR1, NPAR1 = sections([("g_ffn1", DK), ("g_mix", DK), ("g_ffn2", DK), ("b_gate", 2 * DK),
                        ("ln_g", 512), ("ln_b", 512), ("b_s", 512), ("w_s", 512)])
PAR2, NPAR2 = sections([("g_norm", DK), ("b_merge", 4 * DK), ("g_q", 2), ("g_kv", 1), ("b1", 2),
                        ("b2_k", 1), ("pos", 32), ("b2_v", HD)])
FIN, NFIN = sections([("final1", DK), ("final2", DK)])


def build(nc, x_in, w1_in, w2_in, par1_in, par2_in, fin_in, const_in, out):
    ctx = ExitStack()
    with ctx:
        def sb(name, shape):
            return ctx.enter_context(nc.sbuf_tensor(name, shape, F32))

        ring = sb("ring", [P, SLOTS, SLOT])
        w_high = ring[:, :, :].bitcast(BF16).rearrange("p s (n two) -> p s n two", two=2)[:, :, :, 1]
        w_low = ctx.enter_context(nc.sbuf_tensor("w_low", [P, SLOTS, SLOT], F16))
        xT = sb("xT", [P, DK, T])
        hP = ctx.enter_context(nc.sbuf_tensor("hP", [P, DK, 2, T], F16))
        con = sb("con", [P, NCONST])
        par1 = sb("par1", [P, NPAR1])
        par2 = sb("par2", [P, NPAR2])
        fin = sb("fin", [P, NFIN])
        ones = sb("ones", [P, P])
        stat = sb("stat", [P, 3, T])
        WORK = 21500
        work = sb("work", [P, WORK])
        ps = ctx.enter_context(nc.psum_tensor("ps", [P, 8, 512], F32))

        def area(at, *shape):
            n = int(np.prod(shape))
            assert at + n <= WORK, (at, n)
            v = work[:, at:at + n]
            if len(shape) == 2:
                v = v.rearrange("p (a b) -> p a b", a=shape[0])
            if len(shape) == 3:
                v = v.rearrange("p (a b c) -> p a b c", a=shape[0], b=shape[1])
            return v, at + n

        def pairs(at, n):
            v = work[:, at:at + n * T].bitcast(F16).rearrange("p (n s t) -> p n s t", n=n, s=2)
            assert at + n * T <= WORK, at
            return v, at + n * T

        def const(name, h=None):
            a, b = CONST[name]
            v = con[:, a:b]
            return v if h is None else v.rearrange("p (h n) -> p h n", h=h)

        def p1(name):
            a, b = PAR1[name]
            return par1[:, a:b]

        def p2(name):
            a, b = PAR2[name]
            return par2[:, a:b]

        raw, e = area(0, 2, T)
        rope_a, e = area(e, T)
        rope_b, e = area(e, T)
        probs0, e = area(e, 4, PACK)
        probs1, e = area(e, 4, PACK)
        probs = (probs0, probs1)
        probsT, e = area(e, 4, PACK)
        negmax, e = area(e, 2 * TT, 4)
        sums, e = area(e, 2 * TT, 4)
        common = e
        squares, _ = area(0, DK, T)
        normed = squares
        sig, e = area(0, 4, T)
        gated, e = area(e, 4, T)
        z_raw, e = area(e, 2, T)
        assert e <= common
        hidden, e = pairs(common, FK)
        hidden_raw, e = area(e, 2, T)
        silu_g, e = area(e, 2, T)
        uT, e = area(common, 4, T)
        yaT = uT
        rot, e = area(e, 13, T)
        v_tok, e = area(e, TT, 512)
        va_tok, e = area(e, TT, 512)
        wi_tok, e = area(e, TT, 8)
        ybT, e = area(e, 4, T)
        relu, e = area(e, 4, PACK)
        score, e = area(e, PACK)
        top8, e = area(e, 2 * 8)
        keyset, e = area(e, PACK)
        small, e = area(e, 24)
        yaP, e = pairs(e, 4)
        ybP, e = pairs(e, 4)
        z1P, e = pairs(common, DK)
        a_qkT, e = area(common, 4, T)
        c_qkT, e = area(e, 4, T)
        d_qkT, e = area(e, 4, T)
        b_qT, e = area(e, 4, T)
        b_kT, e = area(e, 4, T)
        a_v, e = area(e, TT, BW)
        b_v, e = area(e, TT, BW)
        d_v, e = area(e, TT, BW)
        c_vg, e = area(e, TT, P)
        c_g, e = area(e, TT, 12)
        gateT = []
        for _ in range(4):
            g, e = area(e, 2, T)
            gateT.append(g)
        cmp_hidden, e = area(e, 2, NCMP)
        k_cmpT, e = area(e, NCMP)
        v_cmp, e = area(e, HD)
        cmp_b, e = area(e, 2)
        cmp_m, e = area(e, 8)
        cmp_p, e = area(e, 4 * TT * NCMP)
        keep = e + e % 2
        cqT, e = area(keep, 2, T)
        ckvT, e = area(e, T)
        kpeT, e = area(e, T)
        latent_sq, e = area(e, 3, T)
        latent_r, e = area(e, 2, T)
        cmpT, e = area(e, 2, T)
        cmp_pT, e = area(keep, 4, T)
        stick_a, stick_log = probs0, probs1
        stick_b, e = area(keep, 4, PACK)
        yT = []
        for _ in range(4):
            y, e = area(e, 2, T)
            yT.append(y)
        yP = []
        for _ in range(4):
            y, e = pairs(e, 2)
            yP.append(y)
        z2P, e = pairs(common, DK)

        x_landed = ctx.enter_context(nc.semaphore("x_landed"))
        consts_landed = ctx.enter_context(nc.semaphore("consts_landed"))
        with nc.Block() as block:
            @block.sync
            def _(sp):
                sp.dma_start(xT[:, :, :], x_in).then_inc(x_landed, 16)
                sp.dma_start(con[:, :], const_in).then_inc(consts_landed, 16)
                sp.dma_start(fin[:, :], fin_in).then_inc(consts_landed, 16)
                sp.wait_ge(x_landed, 16)

            @block.vector
            def _(dve):
                nc.vector.memset(ones[:, :], 1.0)

        def product(bank, slot, off, stride, c0, m, rhs, kt, before=None):
            for k in range(kt):
                if before is not None:
                    before(k)
                a = off + k * stride + c0
                nc.tensor.matmul(bank, w_high[:, slot, a:a + m], rhs(k, 0), start=(k == 0), stop=False)
                nc.tensor.matmul(bank, w_high[:, slot, a:a + m], rhs(k, 1), start=False, stop=False)
                mm = nc.tensor.matmul(bank, w_low[:, slot, a:a + m], rhs(k, 0), start=False, stop=(k == kt - 1))
            return mm

        def product_tok(bank, slot, off, stride, c0, n, lhs, kt):
            for k in range(kt):
                a = off + k * stride + c0
                nc.tensor.matmul(bank, lhs(k, 0), w_high[:, slot, a:a + n], start=(k == 0), stop=False)
                nc.tensor.matmul(bank, lhs(k, 0), w_low[:, slot, a:a + n], start=False, stop=False)
                mm = nc.tensor.matmul(bank, lhs(k, 1), w_high[:, slot, a:a + n], start=False, stop=(k == kt - 1))
            return mm

        def product_whole(bank, slot, off, stride, c0, m, rhs, kt, rows=None):
            for k in range(kt):
                r = P if rows is None else rows[k]
                a = off + k * stride + c0
                mm = nc.tensor.matmul(bank, ring[0:r, slot, a:a + m], rhs(k)[0:r],
                                      start=(k == 0), stop=(k == kt - 1))
            return mm

        def h_part(k, part):
            return hP[:, k, part, :]

        def split(chain, dst, src):
            chain.link(nc.vector.tensor_copy(dst[:, :, 0, :], src))
            return nc.vector.tensor_tensor(dst[:, :, 1, :], src, dst[:, :, 0, :], ALU.subtract)

        class Chain:

            def __init__(self, eng, sem):
                self.eng, self.sem, self.n = eng, sem, 0

            def link(self, ins):
                ins.then_inc(self.sem, 1)
                self.n += 1
                self.eng.wait_ge(self.sem, self.n)

            def count(self, ins):
                ins.then_inc(self.sem, 1)
                self.n += 1
                return self.n

        class Layer:

            def __init__(self, stack, steps, per_step, w_in, par, par_in, l, whole=()):
                self.stack, self.sems = stack, {}
                self.steps, self.per_step, self.whole = steps, per_step, whole
                self.starts = np.concatenate([[0], np.cumsum(steps)]).tolist()
                self.tiles_before = np.concatenate([[0], np.cumsum(per_step)]).tolist()
                self.w_in, self.par, self.par_in, self.l = w_in, par, par_in, l
                self.slot_landed = [self.sem(f"slot{j}_landed") for j in range(SLOTS)]

            def sem(self, name):
                if name not in self.sems:
                    self.sems[name] = self.stack.enter_context(nc.semaphore(name))
                return self.sems[name]

            def split_before(self, n):
                return n - sum(m < n for m in self.whole)

            def landed(self, eng, n, i=0):
                eng.wait_ge(self.slot_landed[n % SLOTS], 16 * (n // SLOTS + 1) + 16 * i)

            def split_(self, pe, n, i=0):
                pe.wait_ge(self.sem("steps_split"), self.split_before(n) + 1 + SLOTS * i)

            def rounds(self, n):
                r = 0
                while (self.steps[n:n + SLOTS * (r + 1)] == [self.steps[n]] * (SLOTS * (r + 1))
                       and self.per_step[n - SLOTS:n + SLOTS * r] == [self.per_step[n - SLOTS]] * (SLOTS * (r + 1))
                       and not any(n <= m < n + SLOTS * (r + 1) for m in self.whole)):
                    r += 1
                return r

            def end_stage(self, eng, k):
                eng.drain().then_inc(self.sem("stage_end"), 1)
                eng.wait_ge(self.sem("stage_end"), 3 * k)

            def clear(self):
                nums = [s.num for s in self.sems.values()]
                nc.all_engine_barrier(sems_to_clear=range(min(nums), max(nums) + 1))

        def stream(sp, L):
            sp.dma_start(L.par[:, :], L.par_in[L.l]).then_inc(L.sem("params_landed"), 16)
            n = 0
            while n < len(L.steps):
                r = L.rounds(n) if n >= SLOTS else 0
                size = L.steps[n]
                if r >= 2:
                    per = L.per_step[n - SLOTS]
                    with sp.Fori(0, r) as i:
                        for j in range(SLOTS):
                            sp.wait_ge(L.sem("tiles_done"), L.tiles_before[n + j - SLOTS + 1] + SLOTS * per * i)
                            sp.dma_start(ring[:, (n + j) % SLOTS, 0:size],
                                         L.w_in[L.l, :, bass.ds(L.starts[n + j] + SLOTS * size * i, size)]
                                         ).then_inc(L.slot_landed[(n + j) % SLOTS], 16)
                    n += SLOTS * r
                else:
                    if n >= SLOTS:
                        sp.wait_ge(L.sem("tiles_done"), L.tiles_before[n - SLOTS + 1])
                    sp.dma_start(ring[:, n % SLOTS, 0:size], L.w_in[L.l, :, L.starts[n]:L.starts[n + 1]]
                                 ).then_inc(L.slot_landed[n % SLOTS], 16)
                    n += 1

        def split_stream(pool, L):
            def low(n, size):
                nc.gpsimd.tensor_tensor(w_low[:, n % SLOTS, 0:size], ring[:, n % SLOTS, 0:size],
                                        w_high[:, n % SLOTS, 0:size], ALU.subtract).then_inc(L.sem("steps_split"), 1)

            n = 0
            while n < len(L.steps):
                r = L.rounds(n) if n >= SLOTS else 0
                if r >= 2:
                    with pool.Fori(0, r) as i:
                        for j in range(SLOTS):
                            L.landed(pool, n + j, i)
                            low(n + j, L.steps[n])
                    n += SLOTS * r
                else:
                    if n not in L.whole:
                        L.landed(pool, n)
                        low(n, L.steps[n])
                    n += 1

        def norm_pe(pe, L, name):
            for k in range(DK):
                pe.wait_ge(L.sem("squared_" + name), k + 1)
                mm = nc.tensor.matmul(ps[:, 7, 0:T], ones[:, :], squares[:, k, :], start=(k == 0), stop=(k == DK - 1))
            mm.then_inc(L.sem("summed_" + name), 1)

        def square_act(act, L, name, taken=None):
            for k in range(DK):
                if taken is not None:
                    act.wait_ge(L.sem("dve_took"), taken + k + 1)
                nc.scalar.activation(squares[:, k, :], xT[:, k, :], ACT.Square).then_inc(L.sem("squared_" + name), 1)

        def norm_act(act, L, name, parts=True):
            act.wait_ge(L.sem("mean_" + name), 1)
            nc.scalar.activation(stat[:, 1, :], stat[:, 0, :], ACT.Sqrt).then_inc(L.sem("root_" + name), 1)
            for k in range(DK if parts else 0):
                act.wait_ge(L.sem("normed_" + name), k + 1)
                nc.scalar.activation(hP[:, k, 0, :], normed[:, k, :], ACT.Copy).then_inc(L.sem("high_" + name), 1)

        def norm_dve(dve, L, chain, name, gain, dst, parts=True):
            dve.wait_ge(L.sem("summed_" + name), 1)
            nc.vector.tensor_scalar(stat[:, 0, :], ps[:, 7, 0:T], 1.0 / D, EPS, ALU.mult, ALU.add
                                    ).then_inc(L.sem("mean_" + name), 1)
            dve.wait_ge(L.sem("root_" + name), 1)
            chain.link(nc.vector.reciprocal(stat[:, 2, :], stat[:, 1, :]))

            def low(k):
                dve.wait_ge(L.sem("high_" + name), k + 1)
                nc.vector.tensor_tensor(hP[:, k, 1, :], dst[:, k, :], hP[:, k, 0, :], ALU.subtract
                                        ).then_inc(L.sem("low_" + name), 1)

            for k in range(DK):
                nc.vector.scalar_tensor_tensor(dst[:, k, :], xT[:, k, :], gain[:, k:k + 1], stat[:, 2, :],
                                               ALU.mult, ALU.mult).then_inc(L.sem("normed_" + name), 1)
                if parts and k >= 2:
                    low(k - 2)
            for k in range(DK - 2, DK) if parts else ():
                low(k)

        UP_ROUNDS, UP_REST = FK // SLOTS, FK % SLOTS

        def ffn_pe(pe, L, n0, a0, v0, name):
            done, act_took, dve_took = L.sem("tiles_done"), L.sem("act_took"), L.sem("dve_took")

            def up_step(i, j, first=False):
                s, slot, b = SLOTS * i + j, (n0 + j) % SLOTS, 2 * (j % 2)
                L.split_(pe, n0 + j, i)
                if not first:
                    pe.wait_ge(act_took, a0 + s - 1)
                product(ps[:, b, 0:T], slot, 0, 256, 0, P, h_part, DK, before=row_tile if first and j == 0 else None
                        ).then_inc(done, 1)
                if not first:
                    pe.wait_ge(dve_took, v0 + s - 1)
                product(ps[:, b + 1, 0:T], slot, 0, 256, P, P, h_part, DK).then_inc(done, 1)

            def row_tile(k):
                pe.wait_ge(L.sem("low_" + name), k + 1)

            for j in range(SLOTS):
                up_step(0, j, first=(j < 2))
            with pe.Fori(1, UP_ROUNDS) as i:
                for j in range(SLOTS):
                    up_step(i, j)
            for j in range(UP_REST):
                up_step(UP_ROUNDS, j)

            pe.wait_ge(L.sem("hidden_low_" + name), FK)
            with pe.Fori(0, DK // SLOTS) as i:
                for j in range(SLOTS):
                    L.split_(pe, n0 + FK + j, i)
                    pe.wait_ge(dve_took, v0 + FK - 1 + j + SLOTS * i)
                    product(ps[:, 4 + j % 2, 0:T], (n0 + FK + j) % SLOTS, 0, P, 0, P,
                            lambda k, part: hidden[:, k, part, :], FK).then_inc(done, 1)

        def ffn_act(act, L, t0, v0, name):
            def up_step(i, j, first=False):
                s, b = SLOTS * i + j, 2 * (j % 2)
                act.wait_ge(L.sem("tiles_done"), t0 + 2 * s + 1)
                if not first:
                    act.wait_ge(L.sem("dve_took"), v0 + s - 1)
                nc.scalar.activation(silu_g[:, j % 2, :], ps[:, b, 0:T], ACT.Silu).then_inc(L.sem("act_took"), 1)

            for j in range(SLOTS):
                up_step(0, j, first=(j < 2))
            with act.Fori(1, UP_ROUNDS) as i:
                for j in range(SLOTS):
                    up_step(i, j)
            for j in range(UP_REST):
                up_step(UP_ROUNDS, j)

        def ffn_dve(dve, L, t0, a0, v0, name):
            def up_step(i, j):
                s, b, r = SLOTS * i + j, 2 * (j % 2), j % 2
                dve.wait_ge(L.sem("tiles_done"), t0 + 2 * s + 2)
                dve.wait_ge(L.sem("act_took"), a0 + s + 1)
                nc.vector.tensor_tensor(hidden_raw[:, r, :], silu_g[:, r, :], ps[:, b + 1, 0:T], ALU.mult
                                        ).then_inc(L.sem("dve_took"), 1)
                dve.wait_ge(L.sem("dve_took"), v0 + s + 1)
                nc.vector.tensor_copy(hidden[:, bass.ds(s, 1), 0, :], hidden_raw[:, r:r + 1, :]
                                      ).then_inc(L.sem("hidden_high_" + name), 1)
                dve.wait_ge(L.sem("hidden_high_" + name), s + 1)
                nc.vector.tensor_tensor(hidden[:, bass.ds(s, 1), 1, :], hidden_raw[:, r:r + 1, :],
                                        hidden[:, bass.ds(s, 1), 0, :], ALU.subtract
                                        ).then_inc(L.sem("hidden_low_" + name), 1)

            with dve.Fori(0, UP_ROUNDS) as i:
                for j in range(SLOTS):
                    up_step(i, j)
            for j in range(UP_REST):
                up_step(UP_ROUNDS, j)
            with dve.Fori(0, DK // 2) as c:
                for nt in range(2):
                    dve.wait_ge(L.sem("tiles_done"), t0 + 2 * FK + 2 * c + nt + 1)
                    xs = xT[:, bass.ds(2 * c + nt, 1), :]
                    nc.vector.scalar_tensor_tensor(xs, ps[:, 4 + nt:5 + nt, 0:T], 0.5, xs, ALU.mult, ALU.add
                                                   ).then_inc(L.sem("dve_took"), 1)

        def out_pe(pe, L, n0, v0, zP):
            for n in range(DK):
                if n % 2 == 0:
                    L.split_(pe, n0 + n // 2)
                if n >= 4:
                    pe.wait_ge(L.sem("dve_took"), v0 + n - 3)
                product(ps[:, n % 4, 0:T], (n0 + n // 2) % SLOTS, 0, 256, n % 2 * P, P,
                        lambda k, part: zP[:, k, part, :], DK).then_inc(L.sem("tiles_done"), 1)

        def out_dve(dve, L, t0):
            for n in range(DK):
                dve.wait_ge(L.sem("tiles_done"), t0 + n + 1)
                nc.vector.tensor_tensor(xT[:, n, :], ps[:, n % 4, 0:T], xT[:, n, :], ALU.add
                                        ).then_inc(L.sem("dve_took"), 1)

        def rope_pe(pe, L, r, raw_count, m, swap):
            pe.wait_ge(L.sem("act_took"), raw_count)
            if r >= 2:
                pe.wait_ge(L.sem("turned_taken"), r - 1)
            nc.tensor.matmul(ps[0:m, 6 + r % 2, 0:T], swap, raw[0:m, r % 2, :], start=True, stop=True
                             ).then_inc(L.sem("turned"), 1)

        def rope_dve(dve, L, chain, r, raw_count, m, cos, sin, dst):
            dve.wait_ge(L.sem("act_took"), raw_count)
            chain.link(nc.vector.tensor_tensor(rope_a[0:m, :], raw[0:m, r % 2, :], cos, ALU.mult))
            dve.wait_ge(L.sem("turned"), r + 1)
            nc.vector.tensor_tensor(rope_b[0:m, :], ps[0:m, 6 + r % 2, 0:T], sin, ALU.mult
                                    ).then_inc(L.sem("turned_taken"), 1)
            dve.wait_ge(L.sem("turned_taken"), r + 1)
            chain.link(nc.vector.tensor_tensor(dst, rope_a[0:m, :], rope_b[0:m, :], ALU.add))

        HALVES = ((0, P), (P, PACK))

        def scores_pe(pe, L, u, q, k):
            if u:
                pe.wait_ge(L.sem("scores_taken"), u)
            for h in range(4):
                nc.tensor.matmul(ps[:, h, 0:P], q(h)[:, 0:P], k(h)[:, 0:P], start=True, stop=True)
                mm = nc.tensor.matmul(ps[:, h, P:PACK], q(h)[:, P:T], k(h)[:, 0:T], start=True, stop=True)
            mm.then_inc(L.sem("scores_ready"), 1)

        def turn_pe(pe, L, u):
            pe.wait_ge(L.sem("probs_ready"), u + 1)
            if u:
                pe.wait_ge(L.sem("mixed_taken"), u)
            for h in range(4):
                for a in range(0, PACK, P):
                    mm = nc.tensor.transpose(ps[:, 4 + h, a:a + P], probs[u % 2][:, h, a:a + P], const("ident"))
            mm.then_inc(L.sem("probsT_ready"), 1)

        def mix_pe(pe, L, u, v):
            pe.wait_ge(L.sem("probsT_copied"), u + 1)
            mix_values(v).then_inc(L.sem("mixed"), 1)

        def mix_values(v, heads=range(4)):
            for h in heads:
                o = HD * (h % 2)
                nc.tensor.matmul(ps[o:o + HD, 4 + h // 2, 0:T], v(0, h), probsT[:, h, 0:T], start=True, stop=False)
                mm = nc.tensor.matmul(ps[o:o + HD, 4 + h // 2, P:T], v(1, h), probsT[:, h, T:PACK],
                                      start=False, stop=True)
            return mm

        def exps_act(act, L, u):
            p, m = probs[u % 2], TT * (u % 2)
            act.wait_ge(L.sem("negmax_ready"), u + 1)
            for h in range(4):
                for t, (a, b) in enumerate(HALVES):
                    nc.scalar.activation(p[:, h, a:b], p[:, h, a:b], ACT.Exp, bias=negmax[:, m + t, h:h + 1],
                                         accum_out=sums[:, m + t, h:h + 1]).then_inc(L.sem("exps_ready"), 1)

        def copy_act(act, L, u):
            act.wait_ge(L.sem("probsT_ready"), u + 1)
            nc.scalar.activation(probsT[:, :, :], ps[:, 4:8, 0:PACK], ACT.Copy).then_inc(L.sem("probsT_copied"), 1)

        def max_dve(dve, L, chain, u, scale, bias):
            p, m = probs[u % 2], TT * (u % 2)
            dve.wait_ge(L.sem("scores_ready"), u + 1)
            if u >= 2:
                dve.wait_ge(L.sem("probsT_ready"), u - 1)
            nc.vector.scalar_tensor_tensor(p, ps[:, 0:4, 0:PACK], scale, bias, ALU.mult, ALU.add
                                           ).then_inc(L.sem("scores_taken"), 1)
            dve.wait_ge(L.sem("scores_taken"), u + 1)
            chain.link(nc.vector.reduce_max(negmax[:, m, :], p[:, :, 0:P], AX.X, negate=True))
            nc.vector.reduce_max(negmax[:, m + 1, :], p[:, :, P:PACK], AX.X, negate=True
                                 ).then_inc(L.sem("negmax_ready"), 1)

        def normalise_dve(dve, L, chain, u, gate=None):
            p, s = probs[u % 2], sums[:, TT * (u % 2):TT * (u % 2) + TT, :]
            dve.wait_ge(L.sem("exps_ready"), 8 * u + 8)
            chain.link(nc.vector.reciprocal(s, s))
            if gate is not None:
                chain.link(nc.vector.tensor_tensor(s, s, gate, ALU.mult))
            for t, (a, b) in enumerate(HALVES):
                r = s[:, t, :].rearrange("p (h o) -> p h o", o=1).to_broadcast([P, 4, b - a])
                ins = nc.vector.tensor_tensor(p[:, :, a:b], p[:, :, a:b], r, ALU.mult)
                if t == 0:
                    chain.link(ins)
            ins.then_inc(L.sem("probs_ready"), 1)

        def first_layer(l):
            with ExitStack() as stack:
                L = Layer(stack, STEPS1, TILES1, w1_in, par1, par1_in, l)
                tb = L.tiles_before
                PROJ = len(FFN_STEPS)
                MERGE = PROJ + len(PROJ1_STEPS)
                OUT = MERGE + len(MERGE1_STEPS)
                FFN2 = OUT + len(OUT_STEPS)
                proj_a, proj_v = FK, FK + DK
                merge_a, merge_v = proj_a + sum(PROJ1_TILES), proj_v
                out_v = merge_v + 2 * DK
                ffn2_a, ffn2_v = merge_a + 2 * DK, out_v + DK
                TILES = [(kind, n) for kind in ("u", "va", "q", "k", "qi", "v") for n in range(4)]
                TILES += [("ki", 0), ("wi", 0), ("wi", 1)]
                ROT = {"q": 0, "k": 4, "qi": 8, "ki": 12}
                ropes = [i for i, (kind, _) in enumerate(TILES) if kind in ROT]
                idx_scale = 64 ** -0.5 * 8 ** -0.5

                def head(base, h):
                    return rot[HD * (h % 2):HD * (h % 2) + HD, base + h // 2, :]

                block = stack.enter_context(nc.Block())

                @block.sync
                def _(sp):
                    stream(sp, L)

                @block.gpsimd
                def _(pool):
                    split_stream(pool, L)

                @block.tensor
                def _(pe):
                    pe.wait_ge(L.sem("params_landed"), 16)
                    norm_pe(pe, L, "ffn1")
                    ffn_pe(pe, L, 0, 0, 0, "ffn1")
                    L.end_stage(pe, 1)

                    pe.wait_ge(consts_landed, 32)
                    norm_pe(pe, L, "mix")

                    def row_tile(k):
                        pe.wait_ge(L.sem("low_mix"), k + 1)

                    for i, (kind, n) in enumerate(TILES):
                        s, b = PROJ + (min(i // 2, 12) if kind != "wi" else 13), i % 6
                        slot = s % SLOTS
                        if tb[PROJ] + i == tb[s]:
                            L.split_(pe, s)
                        if i >= 6:
                            pe.wait_ge(L.sem("act_took"), proj_a + i - 5)
                        if kind in ("u", "q", "k", "qi"):
                            mm = product(ps[:, b, 0:T], slot, 0, 256, n % 2 * P, P, h_part, DK,
                                         before=row_tile if i == 0 else None)
                        elif kind == "ki":
                            mm = product(ps[:, b, 0:T], slot, 0, P, 0, P, h_part, DK)
                        else:
                            w = 8 if kind == "wi" else 256
                            mm = product_tok(ps[:, b, 0:w], slot, 0, w, 0, w,
                                             lambda k, part: hP[:, k, part, n % 2 * P:n % 2 * P + P], DK)
                        mm.then_inc(L.sem("tiles_done"), 1)
                        if i - 1 in ropes:
                            rope_pe(pe, L, ropes.index(i - 1), proj_a + i, P, const("swap64"))
                    L.end_stage(pe, 2)

                    for h in range(8):
                        if h >= 4:
                            pe.wait_ge(L.sem("logits_taken"), h - 3)
                        o = HD * (h % 2)
                        nc.tensor.matmul(ps[:, h % 4, 0:P], head(8, h)[:, 0:P], rot[o:o + HD, 12, 0:P],
                                         start=True, stop=True)
                        nc.tensor.matmul(ps[:, h % 4, P:PACK], head(8, h)[:, P:T], rot[o:o + HD, 12, :],
                                         start=True, stop=True).then_inc(L.sem("logits_ready"), 1)
                    pe.wait_ge(L.sem("gate_normed"), 2)
                    for g in range(4):
                        for c in range(TT):
                            mm = nc.tensor.matmul(ps[:, 4 + g, c * P:c * P + P], va_tok[:, c, g * P:g * P + P],
                                                  p1("w_s")[:, g * P:g * P + P], start=True, stop=True)
                    mm.then_inc(L.sem("tokens_mixed"), 1)
                    pe.wait_ge(L.sem("logits_taken"), 8)
                    pe.wait_ge(L.sem("tokens_taken"), 1)
                    scores_pe(pe, L, 0, lambda h: head(0, h), lambda h: head(4, h))
                    scores_pe(pe, L, 1, lambda h: head(0, 4 + h), lambda h: head(4, 4 + h))
                    for u in range(2):
                        turn_pe(pe, L, u)
                        mix_pe(pe, L, u, lambda t, h: v_tok[:, t, (4 * u + h) * HD:(4 * u + h + 1) * HD])
                    L.end_stage(pe, 3)

                    def merge_step(i, jj, first=False):
                        j = SLOTS * i + jj
                        L.split_(pe, MERGE + jj, i)
                        for q, (off, kt, src) in enumerate(((0, 8, hP), (16, 4, yaP), (8, 8, hP), (20, 4, ybP))):
                            if not first:
                                took, base = ("dve_took", merge_v) if q % 2 else ("act_took", merge_a)
                                pe.wait_ge(L.sem(took), base + 2 * j - 3 + q // 2)
                            product(ps[:, 4 * (jj % 2) + q, 0:T], (MERGE + jj) % SLOTS, off * P, P, 0, P,
                                    lambda k, part: src[:, k, part, :], kt).then_inc(L.sem("tiles_done"), 1)

                    for i in range(2):
                        for jj in range(SLOTS):
                            merge_step(i, jj, first=(i == 0 and jj < 2))
                    pe.wait_ge(L.sem("z_ready"), DK)
                    out_pe(pe, L, OUT, out_v, z1P)
                    L.end_stage(pe, 4)

                    norm_pe(pe, L, "ffn2")
                    ffn_pe(pe, L, FFN2, ffn2_a, ffn2_v, "ffn2")
                    L.end_stage(pe, 5)

                @block.scalar
                def _(act):
                    square_act(act, L, "ffn1")
                    norm_act(act, L, "ffn1")
                    ffn_act(act, L, 0, 0, "ffn1")
                    square_act(act, L, "mix", FK)
                    L.end_stage(act, 1)

                    norm_act(act, L, "mix")
                    for i, (kind, n) in enumerate(TILES):
                        act.wait_ge(L.sem("tiles_done"), tb[PROJ] + i + 1)
                        b = i % 6
                        if kind == "u":
                            ins = nc.scalar.activation(uT[:, n, :], ps[:, b, 0:T], ACT.Gelu_apprx_tanh)
                        elif kind == "va":
                            ins = nc.scalar.activation(va_tok[:, n % 2, n // 2 * 256:n // 2 * 256 + 256], ps[:, b, 0:256],
                                                       ACT.Gelu_apprx_tanh)
                        elif kind == "v":
                            ins = nc.scalar.activation(v_tok[:, n % 2, n // 2 * 256:n // 2 * 256 + 256], ps[:, b, 0:256],
                                                       ACT.Copy)
                        elif kind == "wi":
                            ins = nc.scalar.activation(wi_tok[:, n, :], ps[:, b, 0:8], ACT.Copy, scale=idx_scale)
                        else:
                            r = ropes.index(i)
                            if r >= 2:
                                act.wait_ge(L.sem("turned_taken"), r - 1)
                            ins = nc.scalar.activation(raw[:, r % 2, :], ps[:, b, 0:T], ACT.Copy)
                        ins.then_inc(L.sem("act_took"), 1)
                    L.end_stage(act, 2)

                    act.wait_ge(L.sem("gate_variance"), 1)
                    nc.scalar.activation(small[:, 20:22], small[:, 16:18], ACT.Sqrt).then_inc(L.sem("gate_root"), 1)
                    for h in range(8):
                        act.wait_ge(L.sem("logits_ready"), h + 1)
                        if h >= 4:
                            act.wait_ge(L.sem("scored"), 2 * (h - 4) + 2)
                        nc.scalar.activation(relu[:, h % 4, :], ps[:, h % 4, 0:PACK], ACT.Relu
                                             ).then_inc(L.sem("logits_taken"), 1)
                    for u in range(2):
                        exps_act(act, L, u)
                    for u in range(2):
                        copy_act(act, L, u)
                    L.end_stage(act, 3)

                    for j in range(DK):
                        for q in range(2):
                            act.wait_ge(L.sem("tiles_done"), tb[MERGE] + 4 * j + 2 * q + 1)
                            if j >= 2:
                                act.wait_ge(L.sem("dve_took"), merge_v + 2 * j - 3 + q)
                            nc.scalar.activation(sig[:, 2 * (j % 2) + q, :], ps[:, 4 * (j % 2) + 2 * q, 0:T],
                                                 ACT.Sigmoid, bias=p1("b_gate")[:, DK * q + j:DK * q + j + 1]
                                                 ).then_inc(L.sem("act_took"), 1)
                    square_act(act, L, "ffn2", out_v)
                    L.end_stage(act, 4)

                    norm_act(act, L, "ffn2")
                    ffn_act(act, L, tb[FFN2], ffn2_v, "ffn2")
                    L.end_stage(act, 5)

                @block.vector
                def _(dve):
                    chain = Chain(dve, L.sem("dve_chain"))
                    dve.wait_ge(L.sem("params_landed"), 16)
                    norm_dve(dve, L, chain, "ffn1", p1("g_ffn1"), normed)
                    ffn_dve(dve, L, 0, 0, 0, "ffn1")
                    L.end_stage(dve, 1)

                    dve.wait_ge(consts_landed, 32)
                    norm_dve(dve, L, chain, "mix", p1("g_mix"), normed)
                    for r, i in enumerate(ropes):
                        kind, n = TILES[i]
                        rope_dve(dve, L, chain, r, proj_a + i + 1, P, const("cos64"), const("sin64"),
                                 rot[:, ROT[kind] + n, :])
                    L.end_stage(dve, 2)

                    for c in range(TT):
                        chain.link(nc.vector.bn_stats(small[:, 6 * c:6 * c + 6], va_tok[:, c, :]))
                        chain.link(nc.vector.bn_aggr(small[:, 12 + 2 * c:14 + 2 * c], small[:, 6 * c:6 * c + 6]))
                        ins = nc.vector.tensor_scalar(small[:, 16 + c:17 + c], small[:, 13 + 2 * c:14 + 2 * c],
                                                      EPS, None, ALU.add)
                        if c == 0:
                            chain.link(ins)
                    ins.then_inc(L.sem("gate_variance"), 1)
                    ws = p1("w_s").rearrange("p (g t) -> p g t", g=4)
                    chain.link(nc.vector.tensor_tensor(
                        ws, ws, const("upto").rearrange("p (o t) -> p o t", o=1).to_broadcast([P, 4, P]), ALU.mult))
                    dve.wait_ge(L.sem("gate_root"), 1)
                    chain.link(nc.vector.reciprocal(small[:, 18:20], small[:, 20:22]))
                    for c in range(TT):
                        v = va_tok[:, c, :]
                        chain.link(nc.vector.tensor_scalar(v, v, small[:, 12 + 2 * c:13 + 2 * c],
                                                           small[:, 18 + c:19 + c], ALU.subtract, ALU.mult))
                        chain.link(nc.vector.tensor_tensor(v, v, p1("ln_g"), ALU.mult))
                        nc.vector.tensor_tensor(v, v, p1("ln_b"), ALU.add).then_inc(L.sem("gate_normed"), 1)
                    for h in range(8):
                        dve.wait_ge(L.sem("logits_taken"), h + 1)
                        for t, (a, b) in enumerate(HALVES):
                            if h:
                                dve.wait_ge(L.sem("scored"), 2 * (h - 1) + t + 1)
                            nc.vector.scalar_tensor_tensor(
                                score[:, a:b], relu[:, h % 4, a:b], wi_tok[:, t, h:h + 1],
                                (score if h else const("causal"))[:, a:b], ALU.mult, ALU.add
                            ).then_inc(L.sem("scored"), 1)
                    dve.wait_ge(L.sem("tokens_mixed"), 1)
                    bs = p1("b_s").rearrange("p (g t) -> p g t", g=4)
                    chain.link(nc.vector.tensor_tensor(ybT[:, :, 0:P], ps[:, 4:8, 0:P], bs, ALU.add))
                    nc.vector.tensor_tensor(ybT[:, :, P:T], ps[:, 4:8, P:T], bs, ALU.add
                                            ).then_inc(L.sem("tokens_taken"), 1)
                    dve.wait_ge(L.sem("tokens_taken"), 1)
                    chain.link(nc.vector.tensor_tensor(yaT[:, :, :], ybT[:, :, :], uT[:, :, :], ALU.mult))
                    chain.link(split(chain, yaP, yaT[:, :, :]))
                    dve.wait_ge(L.sem("scored"), 16)
                    replaced = [None, None]
                    for _ in range(TOPK // 8):
                        found = []
                        for t, (a, b) in enumerate(HALVES):
                            if replaced[t] is not None:
                                dve.wait_ge(chain.sem, replaced[t])
                            found.append(chain.count(nc.vector.max(top8[:, 8 * t:8 * t + 8], score[:, a:b])))
                        for t, (a, b) in enumerate(HALVES):
                            dve.wait_ge(chain.sem, found[t])
                            replaced[t] = chain.count(nc.vector.match_replace(
                                score[:, a:b], top8[:, 8 * t:8 * t + 8], score[:, a:b], TAKEN))
                    dve.wait_ge(chain.sem, chain.n)
                    chain.link(nc.vector.tensor_scalar(keyset[:, :], score[:, :], 0.5 * TAKEN, NEG,
                                                       ALU.is_gt, ALU.mult))
                    chain.link(nc.vector.tensor_tensor(keyset[:, :], keyset[:, :], const("causal"), ALU.add))
                    bias = keyset[:, :].rearrange("p (o n) -> p o n", o=1).to_broadcast([P, 4, PACK])
                    max_dve(dve, L, chain, 0, HD ** -0.5, bias)
                    max_dve(dve, L, chain, 1, HD ** -0.5, bias)
                    normalise_dve(dve, L, chain, 0)
                    for u in range(2):
                        if u == 1:
                            normalise_dve(dve, L, chain, 1)
                        dve.wait_ge(L.sem("mixed"), u + 1)
                        nc.vector.tensor_copy(ybT[:, 2 * u:2 * u + 2, :], ps[:, 4:6, 0:T]
                                              ).then_inc(L.sem("mixed_taken"), 1)
                        dve.wait_ge(L.sem("mixed_taken"), u + 1)
                        chain.link(split(chain, ybP[:, 2 * u:2 * u + 2, :, :], ybT[:, 2 * u:2 * u + 2, :]))
                    L.end_stage(dve, 3)

                    for j in range(DK):
                        for q in range(2):
                            dve.wait_ge(L.sem("tiles_done"), tb[MERGE] + 4 * j + 2 * q + 2)
                            dve.wait_ge(L.sem("act_took"), merge_a + 2 * j + q + 1)
                            nc.vector.tensor_tensor(gated[:, 2 * (j % 2) + q, :], sig[:, 2 * (j % 2) + q, :],
                                                    ps[:, 4 * (j % 2) + 2 * q + 1, 0:T], ALU.mult
                                                    ).then_inc(L.sem("dve_took"), 1)
                        dve.wait_ge(L.sem("dve_took"), merge_v + 2 * j + 2)
                        z = z_raw[:, j % 2:j % 2 + 1, :]
                        chain.link(nc.vector.tensor_tensor(z, gated[:, 2 * (j % 2):2 * (j % 2) + 1, :],
                                                           gated[:, 2 * (j % 2) + 1:2 * (j % 2) + 2, :], ALU.add))
                        split(chain, z1P[:, j:j + 1, :, :], z).then_inc(L.sem("z_ready"), 1)
                    out_dve(dve, L, tb[OUT])
                    L.end_stage(dve, 4)

                    norm_dve(dve, L, chain, "ffn2", p1("g_ffn2"), normed)
                    ffn_dve(dve, L, tb[FFN2], ffn2_a, ffn2_v, "ffn2")
                    L.end_stage(dve, 5)
            return L

        def second_layer(l):
            with ExitStack() as stack:
                L = Layer(stack, STEPS2, TILES2, w2_in, par2, par2_in, l, whole=WHOLE2)
                tb = L.tiles_before
                MERGE = len(PROJ2_STEPS)
                OUT = MERGE + len(MERGE2_STEPS)
                TILES = []

                def put(step, kind, count, c0, width):
                    for n in range(count):
                        TILES.append((kind, n, step, c0 + (0 if kind in TOKEN else n * width), width))

                TOKEN = ("a_v", "c_vg", "d_v", "b_v")
                put(0, "a_q", 2, 0, P), put(1, "a_k", 2, 0, P), put(2, "a_v", 2, 0, BW), put(3, "a_gate", 2, 0, P)
                put(4, "cq", 1, 0, P), put(4, "cq_rest", 1, P, HD), put(4, "ckv", 1, 192, P), put(4, "kpe", 1, BW, 96)
                put(5, "b_gate", 2, 0, P), put(6, "c_gate", 2, 0, P)
                put(7, "c_q", 2, 0, P), put(8, "c_k", 2, 0, P), put(9, "c_cmp", 2, 0, P), put(10, "c_vg", 2, 0, 140)
                put(11, "d_q", 2, 0, P), put(12, "d_k", 2, 0, P), put(13, "d_v", 2, 0, BW), put(14, "d_gate", 2, 0, P)
                put(15, "b_q", 4, 0, 96), put(15, "b_k", 4, 768, HD), put(15, "b_v", 2, 1024, BW)
                put(16, "hidden", 1, 0, P)
                TILES.append(("hidden", 1, 17, 0, P))
                put(17, "k_cmp", 1, 0, P), put(17, "v_cmp", 1, 0, HD)
                where = {(kind, n): i for i, (kind, n, *_) in enumerate(TILES)}
                took = lambda kind, n=0: where[kind, n] + 1
                ropes = [where["kpe", 0]] + [where["b_q", h] for h in range(4)]
                merge_a, merge_v = len(TILES), 0
                out_v = merge_v + 32
                scale_b = 96 ** -0.5

                def half(src, h):
                    return src[HD * (h % 2):HD * (h % 2) + HD, h // 2, :]

                def twice(src, h):
                    return src[HD * (h % 2):HD * (h % 2) + HD, :]

                block = stack.enter_context(nc.Block())

                @block.sync
                def _(sp):
                    stream(sp, L)

                @block.gpsimd
                def _(pool):
                    split_stream(pool, L)

                @block.tensor
                def _(pe):
                    pe.wait_ge(L.sem("params_landed"), 16)
                    norm_pe(pe, L, "mix")

                    def row_tile(k):
                        pe.wait_ge(L.sem("low_mix"), k + 1)

                    for i, (kind, n, step, c0, w) in enumerate(TILES):
                        b, slot = i % 6, step % SLOTS
                        if i in tb:
                            (L.landed if step in WHOLE2 else L.split_)(pe, step)
                        if i >= 6:
                            pe.wait_ge(L.sem("act_took"), i - 5)
                        if kind == "b_q":
                            pe.wait_ge(L.sem("latents_normed"), 3)
                            mm = product_whole(ps[0:96, b, 0:T], slot, 0, 384, c0, w, lambda k: cqT[:, k, :], 2,
                                               rows=(P, HD))
                        elif kind == "b_k":
                            mm = product_whole(ps[0:HD, b, 0:T], slot, 0, 0, c0, w, lambda k: ckvT, 1)
                        elif kind == "b_v":
                            mm = nc.tensor.matmul(ps[:, b, 0:BW], ckvT[:, n * P:n * P + P], ring[:, slot, c0:c0 + BW],
                                                  start=True, stop=True)
                        elif kind == "hidden":
                            pe.wait_ge(L.sem("act_took"), took("c_cmp", 1))
                            for k in range(16):
                                nc.tensor.matmul(ps[:, b, 0:NCMP], ring[:, slot, k * P:(k + 1) * P],
                                                 cmpT[:, n, 2 * k:2 * k + 16 * (NCMP - 1) + 1:16],
                                                 start=(k == 0), stop=(k == 15))
                            for k in range(16):
                                mm = nc.tensor.matmul(ps[:, b, 16:17], ring[:, slot, k * P:(k + 1) * P],
                                                      p2("pos")[:, 16 * n + k:16 * n + k + 1],
                                                      start=(k == 0), stop=(k == 15))
                        elif kind == "k_cmp":
                            pe.wait_ge(L.sem("act_took"), took("hidden", 0))
                            mm = nc.tensor.matmul(ps[:, b, 0:NCMP], ring[:, slot, 16 * P:17 * P], cmp_hidden[:, 0, :],
                                                  start=True, stop=True)
                        elif kind == "v_cmp":
                            pe.wait_ge(L.sem("act_took"), took("hidden", 1))
                            mm = nc.tensor.matmul(ps[0:NCMP, b, 0:HD], cmp_hidden[:, 1, :],
                                                  ring[:, slot, 17 * P:17 * P + HD], start=True, stop=True)
                        elif kind in TOKEN:
                            mm = product_tok(ps[:, b, 0:w], slot, 0, PROJ2_WIDTHS[step], c0, w,
                                             lambda k, part: hP[:, k, part, n * P:n * P + P], DK)
                        else:
                            mm = product(ps[0:w, b, 0:T], slot, 0, PROJ2_WIDTHS[step], c0, w, h_part, DK,
                                         before=row_tile if i == 0 else None)
                        mm.then_inc(L.sem("tiles_done"), 1)
                        if i - 1 in ropes:
                            rope_pe(pe, L, ropes.index(i - 1), i, 96, con[0:96, CONST["swap96"][0]:CONST["swap96"][1]])
                        if kind == "c_gate" and n == 0:
                            pe.wait_ge(L.sem("latents_squared"), 3)
                            nc.tensor.matmul(ps[:, 7, 0:T], ones[:, :], latent_sq[:, 0, :], start=True, stop=False)
                            nc.tensor.matmul(ps[:, 7, 0:T], ones[0:HD, :], latent_sq[0:HD, 1, :], start=False, stop=True)
                            nc.tensor.matmul(ps[:, 7, T:2 * T], ones[:, :], latent_sq[:, 2, :], start=True, stop=True
                                             ).then_inc(L.sem("latents_summed"), 1)
                    L.end_stage(pe, 1)

                    units = (
                        (lambda h: half(a_qkT, h), lambda h: half(a_qkT[:, 2:4, :], h),
                         lambda t, h: a_v[:, t, h * HD:h * HD + HD]),
                        (lambda h: b_qT[0:96, h, :], lambda h: b_kT[0:96, h, :],
                         lambda t, h: b_v[:, t, h * HD:h * HD + HD]),
                        (lambda h: half(c_qkT, h), lambda h: twice(c_qkT[:, 2, :], h), lambda t, h: c_vg[:, t, 0:HD]),
                        (lambda h: half(c_qkT, h), lambda h: twice(c_qkT[:, 3, :], h), lambda t, h: c_vg[:, t, HD:P]))
                    scores_pe(pe, L, 0, *units[0][:2])
                    scores_pe(pe, L, 1, *units[1][:2])
                    for u in range(2):
                        turn_pe(pe, L, u)
                        scores_pe(pe, L, u + 2, *units[u + 2][:2])
                        mix_pe(pe, L, u, units[u][2])

                    turn_pe(pe, L, 2)
                    pe.wait_ge(L.sem("scores_taken"), 4)
                    for h in range(4):
                        for t in range(TT):
                            a = (h // 2 * TT + t) * NCMP
                            mm = nc.tensor.matmul(ps[:, h % 2, a:a + NCMP], half(c_qkT, h)[:, t * P:t * P + P],
                                                  twice(k_cmpT, h), start=True, stop=True)
                    mm.then_inc(L.sem("cmp_scores"), 1)
                    mix_pe(pe, L, 2, units[2][2])

                    turn_pe(pe, L, 3)
                    pe.wait_ge(L.sem("cmp_shifted"), 1)
                    for h in range(4):
                        q, k = half(d_qkT, h), half(d_qkT[:, 2:4, :], h)
                        nc.tensor.matmul(ps[:, h, 0:T], k[:, 0:P], q, start=True, stop=True)
                        mm = nc.tensor.matmul(ps[:, h, T:PACK], k[:, P:T], q[:, P:T], start=True, stop=True)
                        if h % 2:
                            mm.then_inc(L.sem("stick_scores"), 1)
                    mix_pe(pe, L, 3, units[3][2])

                    pe.wait_ge(L.sem("cmp_probs"), 1)
                    for h in range(4):
                        for t in range(TT):
                            a = (h * TT + t) * NCMP
                            mm = nc.tensor.transpose(ps[0:NCMP, 6 + h // 2, (h % 2 * TT + t) * P:(h % 2 * TT + t + 1) * P],
                                                     cmp_p[:, a:a + NCMP], const("ident"))
                    mm.then_inc(L.sem("cmp_turned"), 1)
                    pe.wait_ge(L.sem("cmp_copied"), 1)
                    pe.wait_ge(L.sem("mixed_taken"), 4)
                    for h in range(4):
                        o = HD * (h % 2)
                        mm = nc.tensor.matmul(ps[o:o + HD, 4 + h // 2, 0:T], v_cmp[0:NCMP, :], cmp_pT[0:NCMP, h, :],
                                              start=True, stop=True)
                    mm.then_inc(L.sem("cmp_mixed"), 1)

                    pe.wait_ge(L.sem("cmp_taken"), 1)
                    for h in range(4):
                        if h % 2 == 0:
                            pe.wait_ge(L.sem("stick_logs"), h // 2 + 1)
                        s = stick_log[:, h, :]
                        nc.tensor.matmul(ps[:, 4 + h, T:PACK], const("later"), s[:, T:PACK], start=True, stop=True)
                        nc.tensor.matmul(ps[:, 4 + h, 0:T], const("later"), s[:, 0:T], start=True, stop=False)
                        mm = nc.tensor.matmul(ps[:, 4 + h, P:T], ones[:, :], s[:, T:PACK], start=False, stop=True)
                        if h % 2:
                            mm.then_inc(L.sem("stick_sums"), 1)
                    for g in range(2):
                        pe.wait_ge(L.sem("stick_probs"), g + 1)
                        mix_values(lambda t, h: d_v[:, t, h * HD:h * HD + HD], heads=(2 * g, 2 * g + 1)
                                   ).then_inc(L.sem("stick_mixed"), 1)
                    L.end_stage(pe, 2)

                    def merge_step(c, br, first=False):
                        L.split_(pe, MERGE + br, c)
                        for nt in range(2):
                            q = 2 * (br % 2) + nt
                            for o, (kt, src, took, base) in enumerate((
                                    (DK, hP, "act_took", merge_a), (2, yP[br], "dve_took", merge_v))):
                                if not first:
                                    pe.wait_ge(L.sem(took), base + 8 * c + 2 * br + nt - 3)
                                product(ps[:, 2 * q + o, 0:T], (MERGE + br) % SLOTS, DK * o * 256, 256, nt * P, P,
                                        lambda k, part: src[:, k, part, :], kt).then_inc(L.sem("tiles_done"), 1)

                    for br in range(4):
                        merge_step(0, br, first=(br < 2))
                    with pe.Fori(1, 4) as c:
                        for br in range(4):
                            merge_step(c, br)
                    pe.wait_ge(L.sem("z_ready"), DK)
                    out_pe(pe, L, OUT, out_v, z2P)
                    L.end_stage(pe, 3)

                @block.scalar
                def _(act):
                    square_act(act, L, "mix")
                    norm_act(act, L, "mix")
                    own = Chain(act, L.sem("act_chain"))
                    for i, (kind, n, step, c0, w) in enumerate(TILES):
                        act.wait_ge(L.sem("tiles_done"), i + 1)
                        src = ps[0:min(w, P), i % 6, 0:T]
                        if kind in ("cq", "cq_rest", "ckv"):
                            j = ("cq", "cq_rest", "ckv").index(kind)
                            nc.scalar.activation(latent_sq[0:w, j, :], src, ACT.Square
                                                 ).then_inc(L.sem("latents_squared"), 1)
                            dst, f = (ckvT if j == 2 else cqT[0:w, j, :]), ACT.Copy
                        elif kind in ("a_q", "a_k", "c_q", "c_k", "d_q", "d_k"):
                            qk = {"a": a_qkT, "c": c_qkT, "d": d_qkT}[kind[0]]
                            dst, f = qk[:, n + 2 * (kind[2] == "k"), :], ACT.Copy
                        elif kind.endswith("gate"):
                            dst, f = gateT["abcd".index(kind[0])][:, n, :], ACT.Silu
                        elif kind == "b_k":
                            dst, f = b_kT[0:HD, n, :], ACT.Copy
                        elif kind in ("a_v", "b_v", "d_v"):
                            dst, f = {"a_v": a_v, "b_v": b_v, "d_v": d_v}[kind][:, n, :], ACT.Copy
                            src = ps[:, i % 6, 0:BW]
                        elif kind == "c_vg":
                            own.link(nc.scalar.activation(c_g[:, n, :], ps[:, i % 6, P:140], ACT.Sigmoid))
                            dst, f, src = c_vg[:, n, :], ACT.Copy, ps[:, i % 6, 0:P]
                        elif kind == "c_cmp":
                            own.link(nc.scalar.activation(cmpT[0:HD, n, :], ps[0:HD, i % 6, 0:T], ACT.Copy))
                            dst, f, src = cmpT[HD:P, n, 0:T - 1], ACT.Copy, ps[HD:P, i % 6, 1:T]
                        elif kind == "hidden":
                            act.wait_ge(L.sem("cmp_bias"), n + 1)
                            nc.scalar.activation(cmp_hidden[:, n, :], ps[:, i % 6, 0:NCMP], ACT.Gelu_apprx_tanh,
                                                 bias=cmp_b[:, n:n + 1]).then_inc(L.sem("act_took"), 1)
                            continue
                        elif kind == "k_cmp":
                            nc.scalar.activation(k_cmpT, ps[:, i % 6, 0:NCMP], ACT.Identity, bias=p2("b2_k")
                                                 ).then_inc(L.sem("act_took"), 1)
                            continue
                        elif kind == "v_cmp":
                            dst, f, src = v_cmp[0:NCMP, :], ACT.Copy, ps[0:NCMP, i % 6, 0:HD]
                        else:
                            r = ropes.index(i)
                            if r >= 2:
                                act.wait_ge(L.sem("turned_taken"), r - 1)
                            dst, f = raw[0:96, r % 2, :], ACT.Copy
                        nc.scalar.activation(dst, src, f).then_inc(L.sem("act_took"), 1)
                        if kind == "c_gate" and n == 1:
                            act.wait_ge(L.sem("latents_mean"), 1)
                            nc.scalar.activation(latent_sq[:, 0:2, :], latent_r, ACT.Sqrt
                                                 ).then_inc(L.sem("latents_root"), 1)
                    L.end_stage(act, 1)

                    exps_act(act, L, 0)
                    exps_act(act, L, 1)
                    for u in range(4):
                        copy_act(act, L, u)
                        if u < 2:
                            exps_act(act, L, u + 2)
                        elif u == 2:
                            act.wait_ge(L.sem("cmp_shifted"), 1)
                            nc.scalar.activation(cmp_p, cmp_p, ACT.Exp).then_inc(L.sem("cmp_exps"), 1)
                    pair = (slice(0, 2), slice(2, 4))
                    for g, hh in enumerate(pair):
                        act.wait_ge(L.sem("stick_scores"), g + 1)
                        nc.scalar.activation(stick_a[:, hh, :], ps[:, hh, 0:PACK], ACT.Abs, scale=HD ** -0.5
                                             ).then_inc(L.sem("stick_abs"), 1)
                    act.wait_ge(L.sem("cmp_turned"), 1)
                    nc.scalar.activation(cmp_pT[0:NCMP, :, :].rearrange("p (b h) t -> p b (h t)", b=2),
                                         ps[0:NCMP, 6:8, :], ACT.Copy).then_inc(L.sem("cmp_copied"), 1)
                    for g, hh in enumerate(pair):
                        act.wait_ge(L.sem("stick_abs"), g + 1)
                        nc.scalar.activation(stick_a[:, hh, :], stick_a[:, hh, :], ACT.Exp, scale=-1.0
                                             ).then_inc(L.sem("stick_decay"), 1)
                    for g, hh in enumerate(pair):
                        act.wait_ge(L.sem("stick_decay"), g + 1)
                        nc.scalar.activation(stick_a[:, hh, :], stick_a[:, hh, :], ACT.Ln, bias=1.0
                                             ).then_inc(L.sem("stick_log1p"), 1)
                    for g, hh in enumerate(pair):
                        act.wait_ge(L.sem("stick_exponent"), g + 1)
                        nc.scalar.activation(probsT[:, hh, :], stick_a[:, hh, :], ACT.Exp
                                             ).then_inc(L.sem("stick_exps"), 1)
                    L.end_stage(act, 2)

                    for m in range(32):
                        c, br, nt = m // 8, m % 8 // 2, m % 2
                        act.wait_ge(L.sem("tiles_done"), tb[MERGE] + 2 * m + 1)
                        if m >= 4:
                            act.wait_ge(L.sem("dve_took"), merge_v + m - 3)
                        j = DK * br + 2 * c + nt
                        nc.scalar.activation(sig[:, m % 4, :], ps[:, 2 * (m % 4), 0:T], ACT.Sigmoid,
                                             bias=p2("b_merge")[:, j:j + 1]).then_inc(L.sem("act_took"), 1)
                    L.end_stage(act, 3)

                @block.vector
                def _(dve):
                    chain = Chain(dve, L.sem("dve_chain"))
                    dve.wait_ge(L.sem("params_landed"), 16)
                    norm_dve(dve, L, chain, "mix", p2("g_norm"), normed)
                    c96, s96 = (con[0:96, CONST[n][0]:CONST[n][1]] for n in ("cos96", "sin96"))
                    rope_dve(dve, L, chain, 0, took("kpe"), 96, c96, s96, kpeT[0:96, :])
                    chain.link(nc.vector.tensor_copy(
                        b_kT[HD:96, :, :], kpeT[HD:96, :].rearrange("p (o t) -> p o t", o=1).to_broadcast([32, 4, T])))
                    dve.wait_ge(L.sem("latents_summed"), 1)
                    chain.link(nc.vector.tensor_scalar(latent_r[:, 0, :], ps[:, 7, 0:T], 1.0 / 192, EPS, ALU.mult, ALU.add))
                    nc.vector.tensor_scalar(latent_r[:, 1, :], ps[:, 7, T:2 * T], 1.0 / P, EPS, ALU.mult, ALU.add
                                            ).then_inc(L.sem("latents_mean"), 1)
                    dve.wait_ge(L.sem("latents_root"), 1)
                    chain.link(nc.vector.reciprocal(latent_r, latent_sq[:, 0:2, :]))
                    for j, (v, w, g) in enumerate(((cqT[:, 0, :], P, p2("g_q")[:, 0:1]),
                                                   (cqT[0:HD, 1, :], HD, p2("g_q")[0:HD, 1:2]), (ckvT, P, p2("g_kv")))):
                        nc.vector.scalar_tensor_tensor(v, v, g, latent_r[0:w, j // 2, :], ALU.mult, ALU.mult
                                                       ).then_inc(L.sem("latents_normed"), 1)
                    for h in range(4):
                        rope_dve(dve, L, chain, 1 + h, took("b_q", h), 96, c96, s96, b_qT[0:96, h, :])
                    for n in range(2):
                        dve.wait_ge(L.sem("tiles_done"), took("hidden", n))
                        nc.vector.tensor_tensor(cmp_b[:, n:n + 1], ps[:, where["hidden", n] % 6, 16:17],
                                                p2("b1")[:, n:n + 1], ALU.add).then_inc(L.sem("cmp_bias"), 1)
                    dve.wait_ge(L.sem("act_took"), took("v_cmp"))
                    chain.link(nc.vector.tensor_tensor(v_cmp[0:NCMP, :], v_cmp[0:NCMP, :], p2("b2_v")[0:NCMP, :], ALU.add))
                    L.end_stage(dve, 1)

                    causal = const("causal").rearrange("p (o n) -> p o n", o=1).to_broadcast([P, 4, PACK])
                    gates = lambda b: c_g[:, :, b::3]
                    kinds = ((HD ** -0.5, const("alibi_a", 4)), (scale_b, causal),
                             (HD ** -0.5, const("alibi_c", 4)), (HD ** -0.5, const("alibi_c", 4)))
                    cp = cmp_p.rearrange("p (h n) -> p h n", h=4)
                    al = const("alibi_cmp", 4)
                    c8 = cmp_p.rearrange("p (g n) -> p g n", g=8)
                    wide = lambda v: v.rearrange("p (g o) -> p g o", o=1).to_broadcast([P, 8, NCMP])

                    def shift_compressed():
                        dve.wait_ge(L.sem("cmp_scores"), 1)
                        for odd in range(2):
                            chain.link(nc.vector.scalar_tensor_tensor(
                                cp[:, odd::2, :], ps[:, odd, 0:4 * NCMP].rearrange("p (h n) -> p h n", h=2), HD ** -0.5,
                                al[:, odd::2, :], ALU.mult, ALU.add))
                        chain.link(nc.vector.reduce_max(cmp_m, c8, AX.X, negate=True))
                        chain.link(nc.vector.tensor_scalar(cmp_m, cmp_m, -0.1 * NEG, None, ALU.min))
                        nc.vector.tensor_tensor(c8, c8, wide(cmp_m), ALU.add).then_inc(L.sem("cmp_shifted"), 1)

                    def take_mixed(u):
                        dve.wait_ge(L.sem("mixed"), u + 1)
                        if u < 2:
                            ins = nc.vector.tensor_tensor(yT[u], ps[:, 4:6, 0:T], gateT[u], ALU.mult)
                        elif u == 2:
                            ins = nc.vector.tensor_copy(yT[2], ps[:, 4:6, 0:T])
                        else:
                            ins = nc.vector.tensor_tensor(yT[2], ps[:, 4:6, 0:T], yT[2], ALU.add)
                        ins.then_inc(L.sem("mixed_taken"), 1)
                        dve.wait_ge(L.sem("mixed_taken"), u + 1)
                        if u < 2:
                            chain.link(split(chain, yP[u], yT[u]))

                    max_dve(dve, L, chain, 0, *kinds[0])
                    max_dve(dve, L, chain, 1, *kinds[1])
                    for u, gate in enumerate((None, None, gates(1), gates(2))):
                        normalise_dve(dve, L, chain, u, gate)
                        if u:
                            take_mixed(u - 1)
                        if u < 2:
                            max_dve(dve, L, chain, u + 2, *kinds[u + 2])
                        elif u == 2:
                            shift_compressed()
                    take_mixed(3)

                    dve.wait_ge(L.sem("cmp_exps"), 1)
                    chain.link(nc.vector.reduce_sum(cmp_m, c8, AX.X))
                    chain.link(nc.vector.tensor_scalar(cmp_m, cmp_m, 1e-30, None, ALU.max))
                    chain.link(nc.vector.reciprocal(cmp_m, cmp_m))
                    chain.link(nc.vector.tensor_tensor(cmp_m.rearrange("p (h t) -> p h t", h=4),
                                                       cmp_m.rearrange("p (h t) -> p h t", h=4),
                                                       gates(0).rearrange("p t h -> p h t"), ALU.mult))
                    nc.vector.tensor_tensor(c8, c8, wide(cmp_m), ALU.mult).then_inc(L.sem("cmp_probs"), 1)
                    dve.wait_ge(L.sem("cmp_mixed"), 1)
                    nc.vector.tensor_tensor(yT[2], ps[:, 4:6, 0:T], yT[2], ALU.add).then_inc(L.sem("cmp_taken"), 1)
                    dve.wait_ge(L.sem("cmp_taken"), 1)
                    chain.link(nc.vector.tensor_tensor(yT[2], yT[2], gateT[2], ALU.mult))
                    chain.link(split(chain, yP[2], yT[2]))

                    before = const("before").rearrange("p (o n) -> p o n", o=1).to_broadcast([P, 2, PACK])
                    pair = (slice(0, 2), slice(2, 4))
                    for g, hh in enumerate(pair):
                        dve.wait_ge(L.sem("stick_abs"), g + 1)
                        chain.link(nc.vector.tensor_scalar(stick_b[:, hh, :], ps[:, hh, 0:PACK], HD ** -0.5, 0.0,
                                                           ALU.mult, ALU.max))
                    for g, hh in enumerate(pair):
                        dve.wait_ge(L.sem("stick_log1p"), g + 1)
                        chain.link(nc.vector.tensor_tensor(stick_b[:, hh, :], stick_b[:, hh, :], stick_a[:, hh, :],
                                                           ALU.add))
                        nc.vector.tensor_tensor(stick_log[:, hh, :], stick_b[:, hh, :], before, ALU.mult
                                                ).then_inc(L.sem("stick_logs"), 1)
                    for g, hh in enumerate(pair):
                        chain.link(nc.vector.scalar_tensor_tensor(stick_a[:, hh, :], ps[:, hh, 0:PACK], HD ** -0.5,
                                                                  stick_b[:, hh, :], ALU.mult, ALU.subtract))
                        dve.wait_ge(L.sem("stick_sums"), g + 1)
                        nc.vector.tensor_tensor(stick_a[:, hh, :], stick_a[:, hh, :],
                                                ps[:, 4 + 2 * g:6 + 2 * g, 0:PACK], ALU.subtract
                                                ).then_inc(L.sem("stick_exponent"), 1)
                    for g, hh in enumerate(pair):
                        dve.wait_ge(L.sem("stick_exps"), g + 1)
                        nc.vector.tensor_tensor(probsT[:, hh, :], probsT[:, hh, :], before, ALU.mult
                                                ).then_inc(L.sem("stick_probs"), 1)
                    for g in range(2):
                        dve.wait_ge(L.sem("stick_mixed"), g + 1)
                        chain.link(nc.vector.tensor_tensor(yT[3][:, g:g + 1, :], ps[:, 4 + g:5 + g, 0:T],
                                                           gateT[3][:, g:g + 1, :], ALU.mult))
                    chain.link(split(chain, yP[3], yT[3]))
                    L.end_stage(dve, 2)

                    for m in range(32):
                        c, br, nt = m // 8, m % 8 // 2, m % 2
                        z = z_raw[:, nt, :]
                        dve.wait_ge(L.sem("tiles_done"), tb[MERGE] + 2 * m + 2)
                        dve.wait_ge(L.sem("act_took"), merge_a + m + 1)
                        nc.vector.tensor_tensor(gated[:, m % 4, :] if br else z, sig[:, m % 4, :],
                                                ps[:, 2 * (m % 4) + 1, 0:T], ALU.mult).then_inc(L.sem("dve_took"), 1)
                        dve.wait_ge(L.sem("dve_took"), merge_v + m + 1)
                        if br:
                            chain.link(nc.vector.tensor_tensor(z, z, gated[:, m % 4, :], ALU.add))
                        if br == 3:
                            split(chain, z2P[:, 2 * c + nt:2 * c + nt + 1, :, :], z_raw[:, nt:nt + 1, :]
                                  ).then_inc(L.sem("z_ready"), 1)
                    out_dve(dve, L, tb[OUT])
                    L.end_stage(dve, 3)
            return L

        def final_norm(name, gain, to_dram):
            with ExitStack() as stack:
                L = Layer(stack, [0], [0], None, None, None, None)
                block = stack.enter_context(nc.Block())

                @block.tensor
                def _(pe):
                    norm_pe(pe, L, name)

                @block.scalar
                def _(act):
                    square_act(act, L, name)
                    norm_act(act, L, name, parts=False)

                @block.vector
                def _(dve):
                    norm_dve(dve, L, Chain(dve, L.sem("dve_chain")), name, gain, area(common, DK, T)[0] if to_dram else xT,
                             parts=False)

                if to_dram:
                    @block.sync
                    def _(sp):
                        sp.wait_ge(L.sem("normed_" + name), DK)
                        sp.dma_start(out, area(common, DK, T)[0]).then_inc(L.sem("out_written"), 16)
                        sp.wait_ge(L.sem("out_written"), 16)
            L.clear()

        def final(name):
            a, b = FIN[name]
            return fin[:, a:b]

        with nc.Fori(0, DEPTH) as l:
            first_layer(l).clear()
        final_norm("final1", final("final1"), False)
        with nc.Fori(0, DEPTH) as l:
            second_layer(l).clear()
        final_norm("final2", final("final2"), True)


def rope_tables(half, pad, total):
    if half == HD // 2:
        inv = np.float32(10000.0) ** (-np.arange(0, 2 * half, 2, dtype=np.float32) / np.float32(2 * half))
    else:
        inv = np.float32(10000.0) ** (-np.arange(half, dtype=np.float32) / np.float32(half))
    ang = np.arange(T, dtype=np.float32)[:, None] * inv.astype(np.float32)[None, :]
    c, s = np.cos(ang).T, np.sin(ang).T
    cos = np.concatenate([np.ones((pad, T)), c, c])
    sin = np.concatenate([np.zeros((pad, T)), -s, s])
    swap = np.zeros((pad + 2 * half, pad + 2 * half))
    i = np.arange(half)
    swap[pad + i, pad + half + i] = swap[pad + half + i, pad + i] = 1
    n = total // (pad + 2 * half)
    return np.tile(cos, (n, 1)), np.tile(sin, (n, 1)), np.kron(np.eye(n), swap)


def constants():
    c = np.zeros((P, NCONST), np.float32)

    def put(name, v):
        a, b = CONST[name]
        v = np.asarray(v, np.float32)
        c[:v.shape[0], a:b] = v.reshape(v.shape[0], -1)

    put("ident", np.eye(P))
    cos, sin, swap = rope_tables(32, 0, P)
    put("cos64", cos), put("sin64", sin), put("swap64", swap)
    cos, sin, swap = rope_tables(16, 64, 96)
    put("cos96", cos), put("sin96", sin), put("swap96", swap)
    t, s = np.arange(T)[:, None], np.arange(T)[None, :]

    def pack(m):
        return np.concatenate([m[:P, :P], m[P:, :]], axis=1)

    dist = t - s
    put("causal", pack(np.where(dist >= 0, 0.0, NEG)))
    slopes = 2.0 ** -(np.arange(8) + 1.0)
    patterns = sum(((dist >= 0) & (dist <= w) & (dist % d == 0)).astype(int) for w, d in ((128, 1), (512, 4), (2048, 16)))
    log_n = np.where(patterns > 0, np.log(np.maximum(patterns, 1)), NEG)
    put("alibi_a", np.stack([pack(np.where(patterns > 0, log_n - m * dist, NEG)) for m in slopes[0::2]], 1))
    put("alibi_c", np.stack([pack(np.where(dist >= 0, -m * dist, NEG)) for m in slopes[1::2]], 1))
    far = t - (16 * np.arange(NCMP) + 31)[None, :]
    cmp_ = np.stack([np.where(far >= 0, -m * far, NEG) for m in slopes[1::2]], 1)
    put("alibi_cmp", cmp_.reshape(TT, P, 4, NCMP).transpose(1, 2, 0, 3))
    put("upto", np.arange(P)[:, None] <= np.arange(P)[None, :])
    strict = (np.arange(P)[:, None] < np.arange(P)[None, :]).astype(np.float32)
    put("before", np.concatenate([strict, np.ones((P, P)), strict], axis=1))
    put("later", np.arange(P)[:, None] > np.arange(P)[None, :])
    return c


def tiles(w):
    k, c = w.shape
    return w.reshape(k // P, P, c).transpose(1, 0, 2).reshape(P, -1)


def vec(v):
    return v.reshape(-1, P).T


def rows(v):
    return np.broadcast_to(v.reshape(1, -1), (P, v.size))


def lay_out_first(a, l):
    def ffn(gu, down):
        out = []
        for i in range(FK):
            c = slice(P * i, P * i + P)
            out.append(tiles(np.concatenate([gu[:, :FF][:, c], gu[:, FF:][:, c]], axis=1)))
        return out + [tiles(down[:, P * i:P * i + P]) for i in range(DK)]

    w = a["w_in"][l]
    u, va, q, k, v = (w[:, 512 * i:512 * i + 512] for i in range(5))
    qi, ki, wi, ga, gb = (w[:, x:y] for x, y in ((2560, 3072), (3072, 3136), (3136, 3144), (3144, 4168), (4168, 5192)))
    steps = ffn(a["ffn1_w_gu"][l], a["ffn1_w_down"][l])
    steps += [tiles(x[:, c:c + 256]) for x in (u, va, q, k, qi, v) for c in (0, 256)]
    steps += [tiles(np.concatenate([ki, ki], 1)), tiles(wi)]
    for i in range(DK):
        c = slice(P * i, P * i + P)
        steps.append(np.concatenate([tiles(x[:, c]) for x in (ga, gb, a["w_pa"][l], a["w_pb"][l])], axis=1))
    steps += [tiles(a["w_out"][l][:, 256 * i:256 * i + 256]) for i in range(4)]
    steps += ffn(a["ffn2_w_gu"][l], a["ffn2_w_down"][l])
    assert [s.shape[1] for s in steps] == STEPS1
    par = np.concatenate([vec(a["ffn1_norm"][l]), vec(a["mix_norm"][l]), vec(a["ffn2_norm"][l]), vec(a["b_gate"][l]),
                          rows(a["gmlp_ln_g"][l]), rows(a["gmlp_ln_b"][l]), rows(a["gmlp_b_s"][l]),
                          a["gmlp_w_s"][l].transpose(2, 0, 1).reshape(P, -1)], axis=1)
    return np.concatenate(steps, axis=1), par


def lay_out_second(a, l):
    a = {name[:-2]: v for name, v in a.items() if name.endswith("_2")}
    w, at, cols = a["w_in"][l], 0, {}
    for name, n in (("a_q", 256), ("a_k", 256), ("a_v", 256), ("a_gate", 256), ("b_cq", 192), ("b_ckv", 128),
                    ("b_kpe", 32), ("b_gate", 256), ("c_q", 256), ("kc", 64), ("vc", 64), ("ks", 64), ("vs", 64),
                    ("kw", 64), ("vw", 64), ("c_g", 12), ("c_gate", 256), ("d_q", 256), ("d_k", 256), ("d_v", 256),
                    ("d_gate", 256)):
        cols[name] = w[:, at:at + n]
        at += n
    assert at == w.shape[1]
    steps = [tiles(np.concatenate([cols[n] for n in names.split()], axis=1)) for names in (
        "a_q", "a_k", "a_v", "a_gate", "b_cq b_ckv b_kpe", "b_gate", "c_gate", "c_q", "ks ks kw kw", "kc kc vc vc",
        "vs vw c_g", "d_q", "d_k", "d_v", "d_gate")]
    uq = np.concatenate([a["mla_w_uq"][l], np.zeros((64, 384), np.float32)])
    ukv = a["mla_w_ukv"][l].reshape(P, 4, P)
    steps.append(np.concatenate([tiles(uq), ukv[:, :, :HD].reshape(P, -1), ukv[:, :, HD:].reshape(P, -1)], axis=1))
    w2 = a["nsa_w2"][l]
    steps.append(tiles(a["nsa_w1"][l, 0]))
    steps.append(np.concatenate([tiles(a["nsa_w1"][l, 1]), w2[0], w2[0], w2[1], np.zeros((P, HD), np.float32)], axis=1))
    for c in range(4):
        cs = slice(256 * c, 256 * c + 256)
        steps += [np.concatenate([tiles(a["w_merge"][l, i][:, cs]), tiles(a["w_branch"][l, i][:, cs])], axis=1)
                  for i in range(4)]
    steps += [tiles(a["w_out"][l][:, 256 * i:256 * i + 256]) for i in range(4)]
    assert [s.shape[1] for s in steps] == STEPS2, [s.shape[1] for s in steps]
    pad = np.zeros(64, np.float32)
    par = np.concatenate([vec(a["norm_g"][l]), vec(a["b_merge"][l].reshape(-1)),
                          vec(np.concatenate([a["mla_q_norm"][l], pad])), vec(a["mla_kv_norm"][l]),
                          a["nsa_b1"][l].T, vec(np.tile(a["nsa_b2"][l, 0], 2)),
                          a["nsa_pos"][l].reshape(32, P).T, rows(a["nsa_b2"][l, 1])], axis=1)
    return np.concatenate(steps, axis=1), par


def kernel(**inputs):
    import concourse.bacc as bacc
    from concourse.bass_utils import run_bass_kernel_spmd

    a = {name: np.asarray(v) for name, v in inputs.items()}
    w1, par1 = (np.ascontiguousarray(np.stack(v)) for v in zip(*(lay_out_first(a, l) for l in range(DEPTH))))
    w2, par2 = (np.ascontiguousarray(np.stack(v)) for v in zip(*(lay_out_second(a, l) for l in range(DEPTH))))
    arrays = {
        "x": np.ascontiguousarray(a["x"][0].T.reshape(DK, P, T).transpose(1, 0, 2)),
        "w1": w1, "w2": w2, "par1": par1, "par2": par2,
        "fin": np.concatenate([vec(a["final_norm"]), vec(a["final_norm_g_2"])], axis=1),
        "const": constants(),
    }
    arrays = {f"in_{name}": np.ascontiguousarray(v) for name, v in arrays.items()}
    nc = bacc.Bacc("TRN2", target_bir_lowering=False, num_devices=1)
    aps = [nc.dram_tensor(n, v.shape, F32, kind="ExternalInput").ap() for n, v in arrays.items()]
    out = nc.dram_tensor("out_0", [P, DK, T], F32, kind="ExternalOutput").ap()
    build(nc, *aps, out)
    r = run_bass_kernel_spmd(nc, [arrays], core_ids=[0])
    got = np.asarray(r.results[0]["out_0"])
    return got.transpose(1, 0, 2).reshape(D, T).T.reshape(1, T, D)
```
